# Optimizing a Trainium2 kernel written in Bass

```python
import jax, jax.numpy as jnp
from jax import lax
import numpy as np

D_MODEL = 1024
BATCH = 1
SEQ = 256
DEPTH = 2

GRID_W = 64
CTX_LEN = 256
N_MIXERS = 2
EXPAND = 2
D_INNER = EXPAND * D_MODEL
HG_HEAD_DIM = 128
HG_HEADS = D_INNER // HG_HEAD_DIM
HG_CHUNK = 32
N_HG_LAYERS = (DEPTH + 1) // 2
MLA_NOPE_DIM = 128
MLA_ROPE_DIM = 64
MLA_V_DIM = 128
MLA_HEADS = D_INNER // MLA_V_DIM
MLA_Q_RANK = D_MODEL // 4
MLA_KV_RANK = D_MODEL // 8
MLA_SCALE = (MLA_NOPE_DIM + MLA_ROPE_DIM) ** -0.5
N_MLA_LAYERS = DEPTH // 2
ROPE_THETA = 10000.0
ROPE_AXIS_DIM = MLA_ROPE_DIM // 2
Q_BLOCK = 128
NORM_EPS = 1e-6


def _rmsnorm(x, g):
    xf = x.astype(jnp.float32)
    y = xf * lax.rsqrt(jnp.mean(xf * xf, axis=-1, keepdims=True) + NORM_EPS)
    return (y * g.astype(jnp.float32)).astype(x.dtype)

def _axial_rope(n_tokens):
    rows = n_tokens // GRID_W
    row = jnp.repeat(jnp.arange(rows, dtype=jnp.float32), GRID_W)
    col = jnp.tile(jnp.arange(GRID_W, dtype=jnp.float32), rows)
    inv = ROPE_THETA ** (-jnp.arange(0, ROPE_AXIS_DIM, 2, dtype=jnp.float32) / ROPE_AXIS_DIM)
    ang = jnp.concatenate([row[:, None] * inv, col[:, None] * inv], axis=-1)
    return jnp.cos(ang), jnp.sin(ang)

def _apply_rope(x, cos, sin):
    half = x.shape[-1] // 2
    x1 = x[..., :half].astype(jnp.float32)
    x2 = x[..., half:].astype(jnp.float32)
    return jnp.concatenate([x1 * cos - x2 * sin, x1 * sin + x2 * cos], axis=-1).astype(x.dtype)

def _hgrn2_scan(q, k, v, log_f, s0):
    B, L, H, _ = q.shape
    DV = v.shape[-1]
    n = L // HG_CHUNK

    def chunks(t):
        return jnp.moveaxis(t.astype(jnp.float32).reshape(B, n, HG_CHUNK, H, t.shape[-1]), 1, 0)

    tri = jnp.tril(jnp.ones((HG_CHUNK, HG_CHUNK), dtype=bool))[None, :, :, None, None]

    def step(S, xs):
        qc, kc, vc, lfc = xs
        b = jnp.cumsum(lfc, axis=1)
        b_last = b[:, -1]
        o_inter = jnp.einsum('bthk,bhkv->bthv', qc * jnp.exp(b), S)
        decay = jnp.exp(jnp.where(tri, b[:, :, None] - b[:, None, :], -jnp.inf))
        scores = jnp.einsum('bthk,btshk,bshk->bhts', qc, decay, kc)
        o_intra = jnp.einsum('bhts,bshv->bthv', scores, vc)
        S_new = jnp.exp(b_last)[..., None] * S + jnp.einsum(
            'bshk,bshv->bhkv', kc * jnp.exp(b_last[:, None] - b), vc)
        return S_new, o_inter + o_intra

    S, o = lax.scan(step, s0, (chunks(q), chunks(k), chunks(v), chunks(log_f)))
    return jnp.moveaxis(o, 0, 1).reshape(B, L, H, DV), S

def _hgrn2_bidir(q, v, gates, init_states):
    (k_f, lf_f), (k_b, lf_b) = gates
    rev = lambda t: jnp.flip(t, axis=1)
    o_f, s_f = _hgrn2_scan(q, k_f, v, lf_f, init_states[0])
    o_b, s_b = _hgrn2_scan(rev(q), rev(k_b), rev(v), rev(lf_b), init_states[1])
    return o_f + rev(o_b), (s_f, s_b)

def _hgrn2_mixer(h_lat, h_ctx, w_in, lb, o_gain, w_out):
    def project(h):
        B, L, _ = h.shape
        heads = lambda t: t.reshape(B, L, HG_HEADS, HG_HEAD_DIM)
        q, i_in, f_fw, f_bw, z = jnp.split(h @ w_in, 5, axis=-1)
        gates = []
        for d, g in enumerate((f_fw, f_bw)):
            lbd = lb[d]
            gf = g.astype(jnp.float32)
            log_f = jnp.logaddexp(jnp.log(lbd), jnp.log1p(-lbd) + jax.nn.log_sigmoid(gf))
            k = (1.0 - lbd) * jax.nn.sigmoid(-gf)
            gates.append((heads(k), heads(log_f)))
        return heads(jax.nn.silu(q)), heads(i_in), gates, z

    def readout(o, z):
        B, L = o.shape[:2]
        o = _rmsnorm(o, o_gain).reshape(B, L, D_INNER).astype(z.dtype)
        return (o * jax.nn.silu(z)) @ w_out

    Bsz = h_lat.shape[0]
    s0 = jnp.zeros((Bsz, HG_HEADS, HG_HEAD_DIM, HG_HEAD_DIM), jnp.float32)
    q_c, v_c, gates_c, z_c = project(h_ctx)
    o_c, ctx_states = _hgrn2_bidir(q_c, v_c, gates_c, (s0, s0))
    q_l, v_l, gates_l, z_l = project(h_lat)
    o_l, _ = _hgrn2_bidir(q_l, v_l, gates_l, ctx_states)
    return readout(o_l, z_l), readout(o_c, z_c)

def _attend(q_nope, q_pe, k_nope, k_pe, v):
    s = (jnp.einsum('bqhd,bkhd->bhqk', q_nope, k_nope, preferred_element_type=jnp.float32)
         + jnp.einsum('bqhr,bkr->bhqk', q_pe, k_pe, preferred_element_type=jnp.float32))
    p = jax.nn.softmax(s * MLA_SCALE, axis=-1)
    return jnp.einsum('bhqk,bkhd->bqhd', p.astype(v.dtype), v)

def _blocked_attend(q_nope, q_pe, k_nope, k_pe, v):
    B, L, H, _ = q_nope.shape
    n = L // Q_BLOCK
    blk = lambda t: jnp.moveaxis(t.reshape(B, n, Q_BLOCK, H, t.shape[-1]), 1, 0)
    o = lax.map(lambda qs: _attend(qs[0], qs[1], k_nope, k_pe, v), (blk(q_nope), blk(q_pe)))
    return jnp.moveaxis(o, 0, 1).reshape(B, L, H, v.shape[-1])

def _mla_mixer(h_lat, h_ctx, w_in, qa_norm, w_qb, kva_norm, w_kvb, w_out, cos, sin, need_ctx):
    splits = [MLA_Q_RANK, MLA_Q_RANK + MLA_KV_RANK, MLA_Q_RANK + MLA_KV_RANK + MLA_ROPE_DIM]

    def queries(q_a):
        B, L, _ = q_a.shape
        q = (_rmsnorm(q_a, qa_norm) @ w_qb).reshape(B, L, MLA_HEADS, MLA_NOPE_DIM + MLA_ROPE_DIM)
        return q[..., :MLA_NOPE_DIM], q[..., MLA_NOPE_DIM:]

    def keys_values(kv_a):
        B, L, _ = kv_a.shape
        kv = (_rmsnorm(kv_a, kva_norm) @ w_kvb).reshape(B, L, MLA_HEADS, MLA_NOPE_DIM + MLA_V_DIM)
        return kv[..., :MLA_NOPE_DIM], kv[..., MLA_NOPE_DIM:]

    def readout(o, z):
        B, L = o.shape[:2]
        return (o.reshape(B, L, D_INNER) * jax.nn.silu(z)) @ w_out

    q_a, kv_a, k_pe, z = jnp.split(h_lat @ w_in, splits, axis=-1)
    q_nope, q_pe = queries(q_a)
    q_pe = _apply_rope(q_pe, cos[None, :, None, :], sin[None, :, None, :])
    k_pe = _apply_rope(k_pe, cos[None], sin[None])
    k_nope, v = keys_values(kv_a)

    if need_ctx:
        qc_a, kvc_a, kc_pe, z_c = jnp.split(h_ctx @ w_in, splits, axis=-1)
    else:
        kvc_a, kc_pe = jnp.split(h_ctx @ w_in[:, splits[0]:splits[2]], [MLA_KV_RANK], axis=-1)
    kc_nope, v_c = keys_values(kvc_a)

    o_lat = _blocked_attend(q_nope, q_pe,
                            jnp.concatenate([kc_nope, k_nope], axis=1),
                            jnp.concatenate([kc_pe, k_pe], axis=1),
                            jnp.concatenate([v_c, v], axis=1))
    y_lat = readout(o_lat, z)
    y_ctx = None
    if need_ctx:
        qc_nope, qc_pe = queries(qc_a)
        y_ctx = readout(_attend(qc_nope, qc_pe, kc_nope, kc_pe, v_c), z_c)
    return y_lat, y_ctx

def first_inputs(seed: int = 0) -> dict:
    key = jax.random.key(seed)
    ks = jax.random.split(key, 20)
    f32 = jnp.float32

    def w(k, shape, fan_in):
        return jax.random.normal(k, shape, f32) * fan_in ** -0.5

    def gain(k, shape):
        return 1.0 + 0.1 * jax.random.normal(k, shape, f32)

    mla_in = MLA_Q_RANK + MLA_KV_RANK + MLA_ROPE_DIM + D_INNER
    return {
        "x": jax.random.normal(ks[0], (BATCH, SEQ, D_MODEL), f32),
        "c": jax.random.normal(ks[1], (BATCH, D_MODEL), f32),
        "ctx": jax.random.normal(ks[2], (BATCH, CTX_LEN, D_MODEL), f32),
        "c_ctx": jax.random.normal(ks[3], (D_MODEL,), f32),
        "ada_w": w(ks[4], (DEPTH, D_MODEL, 3 * D_MODEL), D_MODEL),
        "ada_b": 0.02 * jax.random.normal(ks[5], (DEPTH, 3 * D_MODEL), f32),
        "norm_pre": gain(ks[6], (DEPTH, D_MODEL)),
        "norm_post": gain(ks[7], (DEPTH, D_MODEL)),
        "hg_w_in": w(ks[8], (N_HG_LAYERS, D_MODEL, 5 * D_INNER), D_MODEL),
        "hg_lb_logits": jax.random.normal(ks[9], (N_HG_LAYERS, 2, D_INNER), f32),
        "hg_o_norm": gain(ks[10], (N_HG_LAYERS, HG_HEAD_DIM)),
        "hg_w_out": w(ks[11], (N_HG_LAYERS, D_INNER, D_MODEL), D_INNER),
        "mla_w_in": w(ks[12], (N_MLA_LAYERS, D_MODEL, mla_in), D_MODEL),
        "mla_qa_norm": gain(ks[13], (N_MLA_LAYERS, MLA_Q_RANK)),
        "mla_w_qb": w(ks[14], (N_MLA_LAYERS, MLA_Q_RANK, MLA_HEADS * (MLA_NOPE_DIM + MLA_ROPE_DIM)), MLA_Q_RANK),
        "mla_kva_norm": gain(ks[15], (N_MLA_LAYERS, MLA_KV_RANK)),
        "mla_w_kvb": w(ks[16], (N_MLA_LAYERS, MLA_KV_RANK, MLA_HEADS * (MLA_NOPE_DIM + MLA_V_DIM)), MLA_KV_RANK),
        "mla_w_out": w(ks[17], (N_MLA_LAYERS, D_INNER, D_MODEL), D_INNER),
    }

def first_block(x, c, ctx, c_ctx, ada_w, ada_b, norm_pre, norm_post,
              hg_w_in, hg_lb_logits, hg_o_norm, hg_w_out,
              mla_w_in, mla_qa_norm, mla_w_qb, mla_kva_norm, mla_w_kvb, mla_w_out):
    cos, sin = _axial_rope(x.shape[1])
    p = jax.nn.softmax(hg_lb_logits.astype(jnp.float32), axis=0)
    lower_bounds = jnp.cumsum(p, axis=0) - p[0:1]
    silu_c = jax.nn.silu(c)
    silu_cc = jax.nn.silu(c_ctx)
    x_lat, x_ctx = x, ctx
    for i in range(DEPTH):
        need_ctx = i < DEPTH - 1
        j = i // N_MIXERS
        mod_lat = (silu_c @ ada_w[i] + ada_b[i])[:, None, :]
        mod_ctx = silu_cc @ ada_w[i] + ada_b[i]
        sh_l, sc_l, gt_l = jnp.split(mod_lat, 3, axis=-1)
        sh_c, sc_c, gt_c = jnp.split(mod_ctx, 3, axis=-1)
        h_lat = _rmsnorm(x_lat, norm_pre[i]) * (1.0 + sc_l) + sh_l
        h_ctx = _rmsnorm(x_ctx, norm_pre[i]) * (1.0 + sc_c) + sh_c
        if i % N_MIXERS == 0:
            y_lat, y_ctx = _hgrn2_mixer(h_lat, h_ctx, hg_w_in[j], lower_bounds[j],
                                        hg_o_norm[j], hg_w_out[j])
        else:
            y_lat, y_ctx = _mla_mixer(h_lat, h_ctx, mla_w_in[j], mla_qa_norm[j], mla_w_qb[j],
                                      mla_kva_norm[j], mla_w_kvb[j], mla_w_out[j],
                                      cos, sin, need_ctx)
        x_lat = x_lat + gt_l * _rmsnorm(y_lat, norm_post[i])
        if need_ctx:
            x_ctx = x_ctx + gt_c * _rmsnorm(y_ctx, norm_post[i])
    return x_lat


N_Q_HEADS = 8
N_KV_HEADS = 2
HEAD_DIM = 64
Q_PER_KV = N_Q_HEADS // N_KV_HEADS
ATTN_WIDTH = N_Q_HEADS * HEAD_DIM
KV_WIDTH = N_KV_HEADS * HEAD_DIM
WINDOW = 128
BLOCK = 128
ROPE_BASE = 10000.0
POOL_GROUPS = 4
POOL_GROUP_DIM = 64
POOL_WIDTH = POOL_GROUPS * POOL_GROUP_DIM
POOL_WINDOWS = (2, 4, 8, 16)
FOURIER_GROUPS = 4
FOURIER_GROUP_DIM = 64
FOURIER_WIDTH = FOURIER_GROUPS * FOURIER_GROUP_DIM
N_BRANCHES = 3
IN_SPLITS = (KV_WIDTH, 2 * KV_WIDTH, 2 * KV_WIDTH + ATTN_WIDTH,
             2 * KV_WIDTH + ATTN_WIDTH + POOL_WIDTH,
             2 * KV_WIDTH + ATTN_WIDTH + POOL_WIDTH + FOURIER_WIDTH)
IN_WIDTH = 2 * KV_WIDTH + ATTN_WIDTH + POOL_WIDTH + FOURIER_WIDTH + N_BRANCHES * D_MODEL
D_FF = 2816
CONV_WIDTH = 3
N_MOD = 6
EPS = 1e-6
NEG_INF = -1e30


def rms_norm(x, g):
    xf = x.astype(jnp.float32)
    y = xf * lax.rsqrt(jnp.mean(xf * xf, axis=-1, keepdims=True) + EPS)
    return (y * g.astype(jnp.float32)).astype(x.dtype)

def adaln_params(cond, w_mod, b_mod):
    m = jax.nn.silu(cond) @ w_mod + b_mod
    return jnp.split(m[..., None, :], N_MOD, axis=-1)

def modulate(h, shift, scale):
    return h * (1 + scale) + shift

def axial_rope_tables(n_tokens):
    rows = n_tokens // GRID_W
    row = jnp.repeat(jnp.arange(rows, dtype=jnp.int32), GRID_W).astype(jnp.float32)
    col = jnp.tile(jnp.arange(GRID_W, dtype=jnp.int32), rows).astype(jnp.float32)
    n_freq = HEAD_DIM // 4
    inv_freq = ROPE_BASE ** (-jnp.arange(n_freq, dtype=jnp.float32) / n_freq)
    ang = jnp.stack([row[:, None] * inv_freq[None, :], col[:, None] * inv_freq[None, :]], axis=1)
    return jnp.cos(ang), jnp.sin(ang)

def apply_rope(x, cos, sin):
    B, T, H, _ = x.shape
    xr = x.astype(jnp.float32).reshape(B, T, H, 2, 2, HEAD_DIM // 4)
    c = cos[None, :, None, :, :]
    s = sin[None, :, None, :, :]
    x1, x2 = xr[..., 0, :], xr[..., 1, :]
    out = jnp.stack([x1 * c - x2 * s, x2 * c + x1 * s], axis=-2)
    return out.reshape(x.shape).astype(x.dtype)

def sink_column(sink, lead_shape):
    s = sink.astype(jnp.float32).reshape((1, N_KV_HEADS, Q_PER_KV) + (1,) * (len(lead_shape) - 2))
    return jnp.broadcast_to(s, tuple(lead_shape) + (1,))

def latent_attention(q, k, v, kc, vc, sink):
    B, T = q.shape[:2]
    nb = T // BLOCK
    ctx_len = kc.shape[1]
    scale = HEAD_DIM ** -0.5
    qb = q.reshape(B, nb, BLOCK, N_KV_HEADS, Q_PER_KV, HEAD_DIM)

    def band(a):
        a = a.reshape(B, nb, BLOCK, N_KV_HEADS, HEAD_DIM)
        pad = jnp.zeros_like(a[:, :1])
        ap = jnp.concatenate([pad, a, pad], axis=1)
        return jnp.concatenate([ap[:, :-2], ap[:, 1:-1], ap[:, 2:]], axis=2)

    kb, vb = band(k), band(v)
    s_lat = jnp.einsum('bnqhgd,bnkhd->bhgnqk', qb, kb).astype(jnp.float32) * scale
    blk = jnp.arange(nb, dtype=jnp.int32)[:, None]
    qpos = blk * BLOCK + jnp.arange(BLOCK, dtype=jnp.int32)[None, :]
    kpos = (blk - 1) * BLOCK + jnp.arange(3 * BLOCK, dtype=jnp.int32)[None, :]
    rel = kpos[:, None, :] - qpos[:, :, None]
    valid = (jnp.abs(rel) <= WINDOW) & (kpos[:, None, :] >= 0) & (kpos[:, None, :] < T)
    s_lat = jnp.where(valid, s_lat, NEG_INF)
    s_ctx = jnp.einsum('bnqhgd,bchd->bhgnqc', qb, kc).astype(jnp.float32) * scale
    s_all = jnp.concatenate([s_lat, s_ctx, sink_column(sink, s_lat.shape[:-1])], axis=-1)
    p = jax.nn.softmax(s_all, axis=-1)
    p_lat = p[..., :3 * BLOCK].astype(v.dtype)
    p_ctx = p[..., 3 * BLOCK:3 * BLOCK + ctx_len].astype(v.dtype)
    o = (jnp.einsum('bhgnqk,bnkhd->bnqhgd', p_lat, vb)
         + jnp.einsum('bhgnqc,bchd->bnqhgd', p_ctx, vc))
    return o.reshape(B, T, ATTN_WIDTH)

def context_attention(qc, kc, vc, sink):
    B, L = qc.shape[:2]
    scale = HEAD_DIM ** -0.5
    qg = qc.reshape(B, L, N_KV_HEADS, Q_PER_KV, HEAD_DIM)
    s = jnp.einsum('bqhgd,bkhd->bhgqk', qg, kc).astype(jnp.float32) * scale
    s_all = jnp.concatenate([s, sink_column(sink, s.shape[:-1])], axis=-1)
    p = jax.nn.softmax(s_all, axis=-1)[..., :L].astype(vc.dtype)
    o = jnp.einsum('bhgqk,bkhd->bqhgd', p, vc)
    return o.reshape(B, L, ATTN_WIDTH)

def multiscale_pool(u, pool_w, pool_scale):
    B, T = u.shape[:2]
    ug = u.reshape(B, T, POOL_GROUPS, POOL_GROUP_DIM).astype(jnp.float32)
    cs = jnp.concatenate([jnp.zeros_like(ug[:, :1]), jnp.cumsum(ug, axis=1)], axis=1)
    w = jnp.array(POOL_WINDOWS, dtype=jnp.int32)[None, :]
    t = jnp.arange(T, dtype=jnp.int32)[:, None]
    lo = jnp.clip(t - w // 2, 0, T)
    hi = jnp.clip(t - w // 2 + w, 0, T)
    gidx = jnp.arange(POOL_GROUPS, dtype=jnp.int32)[None, :]
    win_sum = cs[:, hi, gidx] - cs[:, lo, gidx]
    cnt = (hi - lo).astype(jnp.float32)[None, :, :, None]
    pooled = (win_sum / cnt - ug).astype(u.dtype)
    y = jnp.einsum('btgc,gcd->btgd', pooled, pool_w).reshape(B, T, POOL_WIDTH)
    return y * pool_scale

def fourier_mix(f):
    B, T = f.shape[:2]
    fg = f.reshape(B, T, FOURIER_GROUPS, FOURIER_GROUP_DIM).astype(jnp.float32)
    y = jnp.fft.fft2(fg, axes=(1, 3), norm='ortho').real
    return y.astype(f.dtype).reshape(B, T, FOURIER_WIDTH)

def merge_branches(o_attn, pool_in, four_in, gate_in, pool_w, pool_scale,
                   w_br_attn, w_br_pool, w_br_four, w_out):
    g_a, g_p, g_f = jnp.split(jax.nn.sigmoid(gate_in), N_BRANCHES, axis=-1)
    y = (g_a * (o_attn @ w_br_attn)
         + g_p * (multiscale_pool(pool_in, pool_w, pool_scale) @ w_br_pool)
         + g_f * (fourier_mix(four_in) @ w_br_four))
    return y @ w_out

def dwconv_centred(u, w):
    T = u.shape[1]
    up = jnp.pad(u, ((0, 0), (1, 1), (0, 0)))
    return up[:, :T] * w[0] + up[:, 1:T + 1] * w[1] + up[:, 2:] * w[2]

def conv_ffn(h, w_up, conv_w, w_down):
    a = dwconv_centred(h @ w_up, conv_w)
    val, gate = jnp.split(a, 2, axis=-1)
    return (val * jax.nn.silu(gate)) @ w_down

def second_inputs(seed: int = 0) -> dict:
    key = jax.random.key(seed)
    ks = jax.random.split(key, 24)
    f32 = jnp.float32
    n = lambda k, shape, s: jax.random.normal(k, shape, f32) * s
    return {
        'x': n(ks[0], (BATCH, SEQ, D_MODEL), 1.0),
        'c': n(ks[1], (BATCH, D_MODEL), 1.0),
        'ctx': n(ks[2], (BATCH, CTX_LEN, D_MODEL), 1.0),
        'c_ctx': n(ks[3], (D_MODEL,), 1.0),
        'w_mod': n(ks[4], (DEPTH, D_MODEL, N_MOD * D_MODEL), 0.5 * D_MODEL ** -0.5),
        'b_mod': n(ks[5], (DEPTH, N_MOD * D_MODEL), 0.02),
        'norm_mix': 1.0 + n(ks[6], (DEPTH, D_MODEL), 0.02),
        'norm_ffn': 1.0 + n(ks[7], (DEPTH, D_MODEL), 0.02),
        'w_in': n(ks[8], (DEPTH, D_MODEL, IN_WIDTH), D_MODEL ** -0.5),
        'attn_sink': n(ks[9], (DEPTH, N_Q_HEADS), 0.5),
        'pool_w': n(ks[10], (DEPTH, POOL_GROUPS, POOL_GROUP_DIM, POOL_GROUP_DIM), POOL_GROUP_DIM ** -0.5),
        'pool_scale': 1.0 + n(ks[11], (DEPTH, POOL_WIDTH), 0.02),
        'w_br_attn': n(ks[12], (DEPTH, ATTN_WIDTH, D_MODEL), ATTN_WIDTH ** -0.5),
        'w_br_pool': n(ks[13], (DEPTH, POOL_WIDTH, D_MODEL), POOL_WIDTH ** -0.5),
        'w_br_four': n(ks[14], (DEPTH, FOURIER_WIDTH, D_MODEL), FOURIER_WIDTH ** -0.5),
        'w_out': n(ks[15], (DEPTH, D_MODEL, D_MODEL), D_MODEL ** -0.5),
        'w_up': n(ks[16], (DEPTH, D_MODEL, 2 * D_FF), D_MODEL ** -0.5),
        'conv_w': n(ks[17], (DEPTH, CONV_WIDTH, 2 * D_FF), CONV_WIDTH ** -0.5),
        'w_down': n(ks[18], (DEPTH, D_FF, D_MODEL), D_FF ** -0.5),
        'norm_final': 1.0 + n(ks[19], (D_MODEL,), 0.02),
    }

def second_block(x, c, ctx, c_ctx, w_mod, b_mod, norm_mix, norm_ffn, w_in, attn_sink, pool_w, pool_scale,
              w_br_attn, w_br_pool, w_br_four, w_out, w_up, conv_w, w_down, norm_final):
    B, T, _ = x.shape
    cos, sin = axial_rope_tables(T)
    xc = ctx
    for l in range(DEPTH):
        last = l == DEPTH - 1
        sh1, sc1, g1, sh2, sc2, g2 = adaln_params(c, w_mod[l], b_mod[l])
        csh1, csc1, cg1, csh2, csc2, cg2 = adaln_params(c_ctx, w_mod[l], b_mod[l])

        h = modulate(rms_norm(x, norm_mix[l]), sh1, sc1)
        hc = modulate(rms_norm(xc, norm_mix[l]), csh1, csc1)
        k, v, q, u, f, gt = jnp.split(h @ w_in[l], IN_SPLITS, axis=-1)
        if last:
            kc, vc = jnp.split(hc @ w_in[l][:, :2 * KV_WIDTH], 2, axis=-1)
        else:
            kc, vc, qc, uc, fc, gtc = jnp.split(hc @ w_in[l], IN_SPLITS, axis=-1)
        L = hc.shape[1]
        q = apply_rope(q.reshape(B, T, N_Q_HEADS, HEAD_DIM), cos, sin)
        k = apply_rope(k.reshape(B, T, N_KV_HEADS, HEAD_DIM), cos, sin)
        v = v.reshape(B, T, N_KV_HEADS, HEAD_DIM)
        kc = kc.reshape(B, L, N_KV_HEADS, HEAD_DIM)
        vc = vc.reshape(B, L, N_KV_HEADS, HEAD_DIM)
        o = latent_attention(q, k, v, kc, vc, attn_sink[l])
        x = x + g1 * merge_branches(o, u, f, gt, pool_w[l], pool_scale[l],
                                    w_br_attn[l], w_br_pool[l], w_br_four[l], w_out[l])
        if not last:
            oc = context_attention(qc.reshape(B, L, N_Q_HEADS, HEAD_DIM), kc, vc, attn_sink[l])
            xc = xc + cg1 * merge_branches(oc, uc, fc, gtc, pool_w[l], pool_scale[l],
                                           w_br_attn[l], w_br_pool[l], w_br_four[l], w_out[l])

        hf = modulate(rms_norm(x, norm_ffn[l]), sh2, sc2)
        x = x + g2 * conv_ffn(hf, w_up[l], conv_w[l], w_down[l])
        if not last:
            hcf = modulate(rms_norm(xc, norm_ffn[l]), csh2, csc2)
            xc = xc + cg2 * conv_ffn(hcf, w_up[l], conv_w[l], w_down[l])
    return rms_norm(x, norm_final)


def setup_inputs(seed=0):
    out = dict(first_inputs(seed))
    for name, value in second_inputs(seed + 1).items():
        if name != "x":
            out[name + "_2"] = value
    return out


def reference(
    x, c, ctx, c_ctx, ada_w, ada_b, norm_pre, norm_post, hg_w_in, hg_lb_logits, hg_o_norm,
    hg_w_out, mla_w_in, mla_qa_norm, mla_w_qb, mla_kva_norm, mla_w_kvb, mla_w_out, c_2, ctx_2,
    c_ctx_2, w_mod_2, b_mod_2, norm_mix_2, norm_ffn_2, w_in_2, attn_sink_2, pool_w_2,
    pool_scale_2, w_br_attn_2, w_br_pool_2, w_br_four_2, w_out_2, w_up_2, conv_w_2, w_down_2,
    norm_final_2,
):
    x = first_block(
        x, c, ctx, c_ctx, ada_w, ada_b, norm_pre, norm_post, hg_w_in, hg_lb_logits, hg_o_norm,
        hg_w_out, mla_w_in, mla_qa_norm, mla_w_qb, mla_kva_norm, mla_w_kvb, mla_w_out,
    )
    return second_block(
        x, c_2, ctx_2, c_ctx_2, w_mod_2, b_mod_2, norm_mix_2, norm_ffn_2, w_in_2, attn_sink_2,
        pool_w_2, pool_scale_2, w_br_attn_2, w_br_pool_2, w_br_four_2, w_out_2, w_up_2,
        conv_w_2, w_down_2, norm_final_2,
    )


_drawn_inputs = setup_inputs


def setup_inputs(seed=0):
    import zlib

    import numpy as np

    out = dict(_drawn_inputs(seed))
    spreads = {}
    factors = {'mla_qa_norm': 2.774,
     'ctx_2': 4.292,
     'norm_mix_2': 8.0,
     'norm_ffn_2': 8.0,
     'attn_sink_2': 8.0,
     'pool_scale_2': 8.0}
    for name, (base, spread) in spreads.items():
        noise = np.random.default_rng([zlib.crc32(name.encode()), seed]).standard_normal(out[name].shape)
        drawn = base * np.exp(spread * noise) if base else spread * noise
        out[name] = __import__('jax').numpy.asarray(drawn.astype(out[name].dtype))
    for name, factor in factors.items():
        out[name] = (out[name] * factor).astype(out[name].dtype)
    return out
```

```python
import concourse.bass as bass
from concourse import mybir
from contextlib import ExitStack, contextmanager
import numpy as np

D = 1024
KT = D // 128
CTX = 256
LAT = 256
T = CTX + LAT
NG = T // 128
EPS = 1e-6

HG_HEADS = 16
PAIRS = HG_HEADS // 2
PC = 2 * T
UNITS = PC // 128
LEVELS = 7

MLA_HEADS = 16
QB_W = 192
KVB_W = 256
MLA_SCALE = float(192) ** -0.5

N_HEADS = 8
ATT_SCALE = float(64) ** -0.5
D_FF = 2816
FT = D_FF // 128


def wait_apart(eng, sem, value):
    if not isinstance(value, int):
        reg = eng.to_reg(value)
        eng.wait_ge(sem, 1)
        eng.wait_ge(sem, reg)
        return
    eng.wait_ge(sem, value)


def raised(n):
    return n + 1


class Steps:

    def __init__(self, eng, sem):
        self.eng, self.sem, self.n = eng, sem, 0

    def mark(self, ins):
        self.n = self.n + 1
        ins.then_inc(self.sem, 1)

    def settle(self):
        self.eng.wait_ge(self.sem, self.n)

    def link(self, ins):
        self.mark(ins)
        self.settle()

    @contextmanager
    def loop(self, first, end, per):
        base = self.n
        with self.eng.Fori(first, end) as i:
            self.n = base + (i - first) * per
            yield i
            if self.max_of(self.n) != base + (end - 1 - first) * per + per:
                raise ValueError(f"a turn links {self.max_of(self.n) - base - (end - 1 - first) * per} steps")
        self.n = base + (end - first) * per

    @staticmethod
    def max_of(v):
        return v if isinstance(v, int) else v.max_val


class Ring:

    WORDS = 12288

    def __init__(self, mem, loaded, used):
        self.mem, self.loaded, self.used = mem, loaded, used
        self.stages, self.count, self.loads = {}, 0, [0] * len(loaded)
        self.last = []

    def stage(self, name, slots, words, turns, parts):
        need = []
        for j in range(slots):
            lo, hi = j * words, (j + 1) * words
            need.append(max([n + 1 for a, b, s, n in self.last if (a < hi and lo < b) or s == j], default=0))
        self.stages[name] = dict(slots=slots, words=words, turns=turns, parts=parts, first=self.count,
                                 loads=list(self.loads), need=need)
        for j in range(slots):
            self.last.append((j * words, (j + 1) * words, j, self.count + slots * (turns - 1) + j))
            self.loads[j] += 16 * parts[j] * turns
        self.count += slots * turns
        if slots * words > self.WORDS:
            raise ValueError("the slots do not fit")

    def slot(self, name, j):
        w = self.stages[name]["words"]
        return self.mem[:, j * w:(j + 1) * w]

    def wait_loaded(self, eng, name, j, turn):
        s = self.stages[name]
        eng.wait_ge(self.loaded[j], s["loads"][j] + 16 * s["parts"][j] * (turn + 1))

    def fill(self, sp, name, copies):
        s = self.stages[name]

        def turn_of(t, first):
            for j in range(s["slots"]):
                need = s["need"][j] if first else s["first"] + s["slots"] * (t - 1) + j + 1
                if not first or need:
                    wait_apart(sp, self.used, need)
                for dst, src in copies(j, t):
                    sp.dma_start(dst, src).then_inc(self.loaded[j], 16)

        turn_of(0, True)
        if s["turns"] > 1:
            with sp.Fori(1, s["turns"]) as t:
                turn_of(t, False)


def build(nc, w, const, out):
    F32, I32 = mybir.dt.float32, mybir.dt.int32
    ALU, ACT, AX = mybir.AluOpType, mybir.ActivationFunctionType, mybir.AxisListType.X
    V, S, PE = nc.vector, nc.scalar, nc.tensor
    ctx = ExitStack()
    with ctx:
        def sb(name, words, dt=F32):
            return ctx.enter_context(nc.sbuf_tensor(name, [128, words], dt))[:, :]

        def sem(name):
            return ctx.enter_context(nc.semaphore(name))

        ps = ctx.enter_context(nc.psum_tensor("ps", [128, 8, 512], F32))[:, :, :]
        STAT = 7

        def view(ap, *dims, at=0):
            return bass.AP(ap.tensor, ap.offset + at, [list(ap.ap[0])] + [list(d) for d in dims])

        xT = sb("xT", KT * T).rearrange("p (k t) -> p k t", k=KT)
        hT = sb("hT", KT * T).rearrange("p (k t) -> p k t", k=KT)
        ring_mem = sb("ring_mem", Ring.WORDS)
        ident = sb("ident", 128)
        ones = {n: sb(f"ones{n}", 128) for n in (1024, 256, 128)}
        VEC = 520
        vecs = sb("vecs", VEC)
        COND, PRE, POST, MIX, FFN, FINAL, OG, QAG, KVG, PSC, ADAB, MODB, CONV = (
            0, 32, 48, 64, 80, 96, 104, 105, 107, 108, 112, 160, 256)
        sil = sb("sil", 32)
        mod_a = [sb(f"mod_a{i}", 48).rearrange("p (m c) -> p m c", c=2) for i in range(2)]
        mod_b = [sb(f"mod_b{i}", 96).rearrange("p (m c) -> p m c", c=2) for i in range(2)]
        coef = sb("coef", 16).rearrange("p (m c) -> p m c", c=2)
        rstd = sb("rstd", T)
        root = sb("root", T)
        sink = sb("sink", 16)

        ARENA = 29100
        arena = sb("arena", ARENA)

        class Place:
            def __init__(self, at=0):
                self.at = at

            def __call__(self, words):
                a, self.at = self.at, self.at + words
                if self.at > ARENA:
                    raise ValueError(f"the arena is {self.at - ARENA} words short")
                return arena[:, a:a + words]

        at = Place()
        x_in = at(4 * D).rearrange("p (g d) -> p g d", g=4)
        v_in = [at(128) for _ in range(6)]

        at = Place()
        oz = at(HG_HEADS * T).rearrange("p (h t) -> p h t", h=HG_HEADS)
        f_st = at(2 * PC).rearrange("p (d c) -> p d c", d=2)
        k_st = at(2 * PC).rearrange("p (d c) -> p d c", d=2)
        q_st = at(PC)
        v_st = at(NG * 256).rearrange("p (g c) -> p g c", g=NG)
        sg = at(2 * T).rearrange("p (b t) -> p b t", b=2)
        Qw, Kw, Tw = at(2 * PC), at(2 * PC), at(2 * PC)
        k_sum = at(PC)
        A_w = at(PC).rearrange("p (u t) -> p u t", u=UNITS)
        v_w = at(NG * 256).rearrange("p (g c) -> p g c", g=NG)
        kTw = at(2 * PC).rearrange("p (d u k) -> p d u k", d=2, u=UNITS)
        St = at(2 * 2 * 3 * 128).rearrange("p (d h s v) -> p d h s v", d=2, h=2, s=3)
        o_sq = k_sum.rearrange("p (h t) -> p h t", h=2)
        masks = at(LEVELS * 128)
        hg_rt, hg_rs = root, rstd
        hg_end = at.at
        o_tmp = sg

        at = Place()
        ozm = at(MLA_HEADS * LAT).rearrange("p (h t) -> p h t", h=MLA_HEADS)
        sgm = at(2 * T).rearrange("p (b t) -> p b t", b=2)
        qa = at(2 * LAT).rearrange("p (k t) -> p k t", k=2)
        kva = at(T)
        kpe = at(T)
        krot = at(LAT)
        sqm = at(3 * T)
        qn = at(2 * LAT).rearrange("p (h t) -> p h t", h=2)
        qpe, qrot = at(LAT), at(LAT)
        kn = at(2 * T).rearrange("p (h t) -> p h t", h=2)
        vm = at(NG * 256).rearrange("p (g c) -> p g c", g=NG)
        Pm = at(4 * T).rearrange("p (b t) -> p b t", b=4)
        PTm = at(2 * NG * LAT).rearrange("p (h g q) -> p h g q", h=2, g=NG)
        stm = at(32).rearrange("p (b n) -> p b n", b=4)
        mla_end = at.at

        at = Place()
        brT = at(8 * T).rearrange("p (k t) -> p k t", k=8)
        yT = at(8 * T).rearrange("p (k t) -> p k t", k=8)
        q_raw = yT[:, 0:4, :]
        kb = at(T)
        k_rot = at(LAT)
        vb = at(NG * 128).rearrange("p (g c) -> p g c", g=NG)
        ub = at(NG * 256).rearrange("p (g c) -> p g c", g=NG)
        fb = at(NG * 256).rearrange("p (g c) -> p g c", g=NG)
        qj = at(T)
        q_rot = at(LAT)
        sc = at(4 * T).rearrange("p (b t) -> p b t", b=4)
        PTb = at(NG * LAT).rearrange("p (g q) -> p g q", g=NG)
        stb = at(32).rearrange("p (b n) -> p b n", b=4)
        fcs = at(2 * T).rearrange("p (b t) -> p b t", b=2)
        b_tables = at.at
        cosb, sinb, rotb = at(LAT), at(LAT), at(128)
        cosm, sinm, rotm = at(LAT), at(LAT), at(128)
        amask = at(2 * T).rearrange("p (g t) -> p g t", g=2)
        poolm = at(2 * 4 * 256).rearrange("p (s g t) -> p s g t", s=2, g=4)
        dftm = at(2 * 512).rearrange("p (s t) -> p s t", s=2)
        dftc = at(256).rearrange("p (a t) -> p a t", a=2)
        poolw = at(512).rearrange("p (l a t) -> p l a t", l=2, a=2)
        pooled = at(2 * T).rearrange("p (b t) -> p b t", b=2)
        gts = at(3 * T).rearrange("p (b t) -> p b t", b=3)
        brg = at(3 * T).rearrange("p (b t) -> p b t", b=3)
        ctx2_in = view(pooled, (D, 2), (1, D))
        at = Place()
        hid = at(FT * T).rearrange("p (f t) -> p f t", f=FT)
        acc = at(4 * T).rearrange("p (b t) -> p b t", b=4)
        sgf = at(2 * T).rearrange("p (b t) -> p b t", b=2)
        o_out = arena[:, 0:2 * D].rearrange("p (g d) -> p g d", g=2)

        loaded = [sem(f"slot{j}_loaded") for j in range(6)]
        strips_used = sem("strips_used")
        x_loaded, ctx2_loaded, vec_loaded, tab_loaded, msk_loaded = sem("x_loaded"), sem("ctx2_loaded"), sem("vec_loaded"), sem("tab_loaded"), sem("msk_loaded")
        dve_step, act_step, pool_step = sem("dve_step"), sem("act_step"), sem("pool_step")
        vec_turned, vec_ready, x_turned, x_copied = sem("vec_turned"), sem("vec_ready"), sem("x_turned"), sem("x_copied")
        rows_kept, mod_turned, coef_ready = sem("rows_kept"), sem("mod_turned"), sem("coef_ready")
        sig_c, sil_ready = sem("sig_c"), sem("sil_ready")
        mod_summed, mod_ready = sem("mod_summed"), sem("mod_ready")
        squared, stat_summed, root_ready, normed, h_ready = (
            sem("squared"), sem("stat_summed"), sem("root_ready"), sem("normed"), sem("h_ready"))
        proj_full, act_freed, dve_freed, sig_ready = sem("proj_full"), sem("act_freed"), sem("dve_freed"), sem("sig_ready")
        kc_ready = sem("kc_ready")
        unpacked, moved, lv_full, lv_free, merged = (
            sem("unpacked"), sem("moved"), sem("lv_full"), sem("lv_free"), sem("merged"))
        kt_full, kt_free, st_full, st_ready, o_full, o_squared, ms_full, rt_ready, o_ready = (
            sem("kt_full"), sem("kt_free"), sem("st_full"), sem("st_ready"), sem("o_full"), sem("o_squared"),
            sem("ms_full"), sem("rt_ready"), sem("o_ready"))
        y_kept, x_added = sem("y_kept"), sem("x_added")
        mp_full, mp_act_kept, mp_dve_kept, rot_full, z_signed, z_kept = (
            sem("mp_full"), sem("mp_act_kept"), sem("mp_dve_kept"), sem("rot_full"), sem("z_signed"), sem("z_kept"))
        s_full, s_max, s_exp, p_ready, pt_full, pt_kept, pv_full, pv_kept = (
            sem("s_full"), sem("s_max"), sem("s_exp"), sem("p_ready"), sem("pt_full"), sem("pt_kept"), sem("pv_full"),
            sem("pv_kept"))
        in_full, in_act_kept, in_dve_kept, qj_ready, k_turned = (
            sem("in_full"), sem("in_act_kept"), sem("in_dve_kept"), sem("qj_ready"), sem("k_turned"))
        br_full, br_act_kept, br_dve_kept = sem("br_full"), sem("br_act_kept"), sem("br_dve_kept")
        mg_full, gates_ready, mg_read, y_ready, out_full = (
            sem("mg_full"), sem("gates_ready"), sem("mg_read"), sem("y_ready"), sem("out_full"))
        tap_ready, conv_ready, sf_ready, hid_ready = sem("tap_ready"), sem("conv_ready"), sem("sf_ready"), sem("hid_ready")
        o_turned, out_kept, out_stored = sem("o_turned"), sem("out_kept"), sem("out_stored")

        ring = Ring(ring_mem, loaded, strips_used)
        ring.stage("ada0", 6, 2048, 2, [1] * 6)
        ring.stage("hg_in", 5, 2048, PAIRS, [1] * 5)
        ring.stage("hg_out", 4, 2048, 2, [1] * 4)
        ring.stage("ada1", 6, 2048, 2, [1] * 6)
        ring.stage("mla_a", 2, 2048, 1, [1, 2])
        ring.stage("mla_z", 4, 2048, 2, [1] * 4)
        ring.stage("mla_b", 2, 1280, PAIRS // 2, [5, 5])
        ring.stage("mla_out", 4, 2048, 2, [1] * 4)
        for l in range(2):
            if l == 0:
                ring.stage("mod0", 6, 2048, 4, [1] * 6)
            ring.stage(f"in{l}", 5, 2048, 1, [1, 4, 4, 1, 1])
            if l == 0:
                ring.stage("mod1", 6, 2048, 4, [1] * 6)
            ring.stage(f"merge{l}", 4, 2048, 4, [1, 1, 1, 4])
            ring.stage(f"out{l}", 4, 2048, 1, [1] * 4)
            ring.stage(f"up{l}", 2, 2048, FT // 2, [2] * 2)
            ring.stage(f"down{l}", 4, FT * 128, 2, [1] * 4)

        NORMS = [("hg_pre", 8), ("hg_post", 8), ("mla_pre", 8), ("qa", 2), ("kva", 1), ("mla_post", 8),
                 ("mix0", 8), ("ffn0", 8), ("mix1", 8), ("ffn1", 8), ("final", 8)]
        norm_no = {name: n for n, (name, _) in enumerate(NORMS)}
        sq_base = {name: sum(k for _, k in NORMS[:n]) for n, (name, _) in enumerate(NORMS)}
        HNORMS = [("hg_pre", 2), ("mla_pre", 2), ("mix0", 2), ("ffn0", 2), ("mix1", 2), ("ffn1", 1)]
        h_no = {name: n for n, (name, _) in enumerate(HNORMS)}
        h_base = {name: 8 * sum(p for _, p in HNORMS[:n]) for n, (name, _) in enumerate(HNORMS)}
        mod_turn = {"ada0": 0, "ada1": 2, "mod0": 4, "mod1": 8}
        h_end = {name: h_base[name] + 8 * p for name, p in HNORMS}

        def norm_scalar(act, name, src, sq, n, between=lambda: None):
            k_n = dict(NORMS)[name]
            for k in range(k_n):
                S.activation(sq(k), src(k), ACT.Square).then_inc(squared, 1)
            between()
            act.wait_ge(stat_summed, norm_no[name] + 1)
            if norm_no[name]:
                act.wait_ge(normed, sq_base[name])
            S.activation(root[:, 0:n], ps[:, STAT, 0:n], ACT.Sqrt, bias=eps).then_inc(root_ready, 1)

        def norm_tensor(pe, name, sq, ones_, n):
            k_n = dict(NORMS)[name]
            if norm_no[name]:
                pe.wait_ge(root_ready, norm_no[name])
            for k in range(k_n):
                pe.wait_ge(squared, sq_base[name] + k + 1)
                mm = PE.matmul(ps[:, STAT, 0:n], ones_, sq(k), start=k == 0, stop=k == k_n - 1)
            mm.then_inc(stat_summed, 1)

        def norm_vector(dve, st, name, n):
            dve.wait_ge(root_ready, norm_no[name] + 1)
            st.link(V.reciprocal(rstd[:, 0:n], root[:, 0:n]))

        def modulate_coef(st, scale, gain):
            V.scalar_tensor_tensor(coef, scale, 1.0, view(gain, (1, 8), (0, 2)), ALU.add, ALU.mult).then_inc(coef_ready, 1)

        def normed_vector(name, src, c0, c1):
            for k in range(8):
                V.tensor_tensor(hT[:, k, c0:c1], src(k), rstd[:, 0:c1 - c0], ALU.mult).then_inc(normed, 1)

        def rows_scalar(act, name, first, end):
            def turn(t):
                for g in range(3):
                    wait_strip(act, name, 2 * g + 1, t)
                    S.activation(mod_rows[0:2, g % 2 * 512:g % 2 * 512 + 512], ps[0:2, 3 + g, :], ACT.Copy).then_inc(rows_kept, 1)

            if end - first == 1:
                turn(first)
            else:
                with act.Fori(first, end) as t:
                    turn(t)

        def modulate_scalar(act, name, shift, halves):
            act.wait_ge(coef_ready, h_no[name] + 1)
            for k in range(8):
                act.wait_ge(normed, sq_base[name] + k + 1)
                for c in halves:
                    cols = slice(c * 256, c * 256 + 256)
                    S.activation(hT[:, k, cols], hT[:, k, cols], ACT.Identity, scale=coef[:, k, c:c + 1],
                                 bias=shift[:, k, c:c + 1]).then_inc(h_ready, 1)

        FINAL_READY = h_base["ffn1"] + 8 + 8
        TAB_ALL = 16 * (1 + 10 + 8)

        rows = lambda ap: ap.rearrange("(k p) -> k p", p=128)
        rows2 = lambda ap: ap.rearrange("l (k p) -> (l k) p", p=128)
        VROWS = (112, 48, 96, 88, 88, 88)
        conv = w["conv_w_2"].rearrange("l c (k p) -> (l c k) p", p=128)
        VSRC = [((0, 0, 8), rows(w["c_ctx"])), ((0, 8, 16), rows2(w["c"])), ((0, 16, 24), rows(w["c_ctx_2"])),
                ((0, 24, 32), rows2(w["c_2"])), ((0, 32, 48), rows2(w["norm_pre"])), ((0, 48, 64), rows2(w["norm_post"])),
                ((0, 64, 80), rows2(w["norm_mix_2"])), ((0, 80, 96), rows2(w["norm_ffn_2"])), ((0, 96, 104), rows(w["norm_final_2"])),
                ((0, 104, 105), w["hg_o_norm"]), ((0, 105, 107), rows2(w["mla_qa_norm"])), ((0, 107, 108), w["mla_kva_norm"]),
                ((0, 108, 112), rows2(w["pool_scale_2"])), ((1, 0, 48), rows2(w["ada_b"])), ((2, 0, 96), rows2(w["b_mod_2"]))]
        VSRC += [((3 + n, 0, 88), conv[88 * n:88 * n + 88, :]) for n in range(3)]
        N_VEC = len(VSRC) + 1

        eps = sb("eps", 1)
        mod_rows = sb("mod_rows", 1024)
        raise_at = sb("raise_at", 10)
        K_c = mod_rows
        masks_i = masks.bitcast(I32).rearrange("p (l t) -> p l t", l=LEVELS)

        block = ctx.enter_context(nc.Block())
        wk = {n: w[n].rearrange("l (k p) n -> l p k n", p=128) for n in
              ("ada_w", "hg_w_in", "hg_w_out", "mla_w_in", "mla_w_qb", "mla_w_kvb", "mla_w_out", "w_mod_2", "w_in_2",
               "w_br_pool_2", "w_br_four_2", "w_out_2", "w_up_2", "w_down_2")}

        def strip(name, j, k):
            return ring.slot(name, j).rearrange("p (k n) -> p k n", k=k)

        HG_ORDER = (2, 3, 0, 4, 1)

        @block.sync
        def _(sp):
            sp.dma_start(x_in[:, 0:2, :], w["ctx"][0].rearrange("(g p) d -> p g d", p=128)).then_inc(x_loaded, 16)
            sp.dma_start(x_in[:, 2:4, :], w["x"][0].rearrange("(g p) d -> p g d", p=128)).then_inc(x_loaded, 16)
            for rows, src in VSRC[1::2]:
                tile_, r0, r1 = rows
                sp.dma_start(v_in[tile_][r0:r1, :], src).then_inc(vec_loaded, 16)
            ring.fill(sp, "ada0", lambda j, t: [(strip("ada0", j, 8), wk["ada_w"][0][:, :, bass.ds(t * 1536 + j * 256, 256)])])
            ring.fill(sp, "hg_in", lambda j, t: [(strip("hg_in", j, 8),
                      wk["hg_w_in"][0][:, :, bass.ds(t * 256 + HG_ORDER[j] * 2048, 256)])])
            ring.fill(sp, "hg_out", lambda j, t: [(strip("hg_out", j, 16), wk["hg_w_out"][0][:, :, bass.ds(t * 512 + j * 128, 128)])])
            ring.fill(sp, "ada1", lambda j, t: [(strip("ada1", j, 8), wk["ada_w"][1][:, :, bass.ds(t * 1536 + j * 256, 256)])])
            mw = wk["mla_w_in"][0]
            ring.fill(sp, "mla_a", lambda j, t: [(strip("mla_a", 0, 8), mw[:, :, 0:256])] if j == 0 else
                      [(strip("mla_a", 1, 8)[:, :, 0:192], mw[:, :, 256:448]),
                       (strip("mla_a", 1, 8)[:, :, 192:256], mw[:, :, 384:448])])
            ring.fill(sp, "mla_z", lambda j, t: [(strip("mla_z", j, 8), mw[:, :, bass.ds(t * 1024 + j * 256 + 448, 256)])])

            def mla_b(j, t):
                nope = ring.slot("mla_b", j)[:, 0:512].rearrange("p (k h c) -> p k h c", k=2, h=2)
                rope = ring.slot("mla_b", j)[:, 512:768].rearrange("p (k h c) -> p k h c", k=2, h=2)
                pair = t * 2 + j
                out_ = []
                for k in range(2):
                    src = wk["mla_w_qb"][0][:, k, bass.ds(pair * (2 * QB_W), 2 * QB_W)].rearrange("p (h c) -> p h c", h=2)
                    out_ += [(nope[:, k], src[:, :, 0:128]), (rope[:, k], src[:, :, 128:192])]
                return out_ + [(ring.slot("mla_b", j)[:, 768:1280], wk["mla_w_kvb"][0][:, 0, bass.ds(pair * (2 * KVB_W), 2 * KVB_W)])]
            ring.fill(sp, "mla_b", mla_b)
            ring.fill(sp, "mla_out", lambda j, t: [(strip("mla_out", j, 16), wk["mla_w_out"][0][:, :, bass.ds(t * 512 + j * 128, 128)])])
            for l in range(2):
                if l == 0:
                    ring.fill(sp, "mod0", lambda j, t: [(strip("mod0", j, 8), wk["w_mod_2"][0][:, :, bass.ds(t * 1536 + j * 256, 256)])])

                def w_in(j, t):
                    s = strip(f"in{l}", j, 8)
                    if j not in (1, 2):
                        return [(s, wk["w_in_2"][l][:, :, j * 256:j * 256 + 256])]
                    s = s.rearrange("p k (n h c) -> p k n h c", n=2, h=2)
                    return [(s[:, :, n, h, :], wk["w_in_2"][l][:, :, 256 + h * 256 + j * 128 - 128 + n * 64:][:, :, 0:64])
                            for n in range(2) for h in range(2)]
                ring.fill(sp, f"in{l}", w_in)
                if l == 0:
                    ring.fill(sp, "mod1", lambda j, t: [(strip("mod1", j, 8), wk["w_mod_2"][1][:, :, bass.ds(t * 1536 + j * 256, 256)])])

                def merge(j, t):
                    if j < 3:
                        return [(strip(f"merge{l}", j, 8), wk["w_in_2"][l][:, :, bass.ds(t * 256 + (1280 + j * 1024), 256)])]
                    s = strip(f"merge{l}", 3, 8)
                    cols = bass.ds(t * 256, 256)
                    a = w["w_br_attn_2"][l].rearrange("(h j p) n -> h p j n", h=2, p=64)
                    return [(s[0:64, 0:4, :], a[0][:, :, cols]), (s[64:128, 0:4, :], a[1][:, :, cols]),
                            (s[:, 4:6, :], wk["w_br_pool_2"][l][:, :, cols]), (s[:, 6:8, :], wk["w_br_four_2"][l][:, :, cols])]
                ring.fill(sp, f"merge{l}", merge)
                ring.fill(sp, f"out{l}", lambda j, t: [(strip(f"out{l}", j, 8), wk["w_out_2"][l][:, :, j * 256:j * 256 + 256])])
                ring.fill(sp, f"up{l}", lambda j, t: [
                    (strip(f"up{l}", j, 8)[:, :, 0:128], wk["w_up_2"][l][:, :, bass.ds((t * 2 + j) * 128, 128)]),
                    (strip(f"up{l}", j, 8)[:, :, 128:256], wk["w_up_2"][l][:, :, bass.ds((t * 2 + j) * 128 + D_FF, 128)])])
                ring.fill(sp, f"down{l}", lambda j, t: [(strip(f"down{l}", j, FT), wk["w_down_2"][l][:, :, bass.ds(t * 512 + j * 128, 128)])])
            for g in range(4):
                sp.wait_ge(out_kept, g + 1)
            sp.dma_start(out[0].rearrange("(g p) d -> p g d", p=128), o_out).then_inc(out_stored, 16)
            sp.wait_ge(out_stored, 16)

        def wait_h(pe, name, k):
            pe.wait_ge(h_ready, h_base[name] + dict(HNORMS)[name] * (k + 1))

        def strip_used(mm):
            mm.then_inc(strips_used, 1)

        def comb(buf, h, u=None):
            n = (PC if u is None else 128) // (2 * h)
            return view(buf, (2 * h, n), (PC + h, 2), (1, h), at=0 if u is None else u * 128)

        def mods_tensor(pe, name, cond, first, end):
            def turned(g, t):
                pe.wait_ge(rows_kept, t * 3 + (mod_turn[name] * 3 + g + 1))
                for m in range(4):
                    col = t * 24 + (g * 8 + m * 2) if isinstance(t, int) else bass.ds(t * 24 + (g * 8 + m * 2), 2)
                    PE.matmul(ps[:, 6, col:col + 2] if isinstance(t, int) else ps[:, 6, col],
                              mod_rows[0:2, g % 2 * 512 + m * 128:g % 2 * 512 + m * 128 + 128], ident[0:2, 0:2],
                              start=True, stop=True).then_inc(mod_turned, 1)

            def turn(t):
                for j in range(6):
                    ring.wait_loaded(pe, name, j, t)
                    wj = strip(name, j, 8)
                    for k in range(8):
                        mm = PE.matmul(ps[0:2, 3 + j // 2, (j % 2) * 256:(j % 2) * 256 + 256], view(sil, (8, 2), at=cond + k), wj[:, k, :],
                                       start=k == 0, stop=k == 7)
                    strip_used(mm)
                    if j in (3, 5):
                        turned(j // 2 - 1, t)
                turned(2, t)

            if end - first == 1:
                turn(first)
            else:
                with pe.Fori(first, end) as t:
                    turn(t)

        def hg_project_tensor(pe, i, idx):
            j, m = divmod(idx, 2)
            if m == 0:
                ring.wait_loaded(pe, "hg_in", j, i)
            n = i * 10 + idx
            first_turn = isinstance(i, int) and i == 0
            if idx in (0, 1):
                if not first_turn:
                    pe.wait_ge(act_freed, i * 6 - 1 + idx)
            elif idx in (2, 3):
                pe.wait_ge(act_freed, i * 6 + idx - 1)
            elif idx in (4, 5):
                pe.wait_ge(act_freed, i * 6 + idx - 1)
            else:
                pe.wait_ge(dve_freed, i * 4 + idx - 5)
            bank = ps[:, idx % 2, :]
            wj = strip("hg_in", j, 8)
            if j < 4:
                for k in range(8):
                    if first_turn and idx == 0:
                        wait_h(pe, "hg_pre", k)
                    mm = PE.matmul(bank, wj[:, k, m * 128:m * 128 + 128], hT[:, k, :], start=k == 0, stop=k == 7)
                if m == 1:
                    strip_used(mm)
                    return
                mm.then_inc(proj_full, 1)
            else:
                for g in range(2):
                    tok = (2 * m + g) * 128
                    for k in range(8):
                        mm = PE.matmul(bank[:, g * 256:g * 256 + 256], hT[:, k, tok:tok + 128], wj[:, k, :],
                                       start=k == 0, stop=k == 7)
                if m == 1:
                    strip_used(mm)
                    return
                mm.then_inc(proj_full, 1)

        def wait_projected(eng, i, idx):
            if idx % 2:
                eng.wait_ge(strips_used, ring.stages["hg_in"]["first"] + i * 5 + (idx + 1) // 2)
            else:
                eng.wait_ge(proj_full, i * 5 + idx // 2 + 1)

        LV = (3, 4)
        KTB = (2, 5)
        STB = (3, 4, 2)
        OB = (6, 7)
        MSB = (5, 3)
        CHAIN = ((1, 0, 3), (0, 1, 2))

        def hg_scores_tensor(pe, i, term):
            if term == 0:
                pe.wait_ge(unpacked, i + 1)
                if not (isinstance(i, int) and i == 0):
                    pe.wait_ge(rt_ready, raised(i * 2))
            else:
                pe.wait_ge(kc_ready, i * LEVELS + term)
            for b in range(2):
                if term:
                    pe.wait_ge(lv_free, i * 16 + 2 * term + b - 1)
                for u in range(4 * b, 4 * b + 4):
                    dst = ps[:, LV[b], (u % 4) * 128:(u % 4) * 128 + 128]
                    if term == 0:
                        mm = PE.matmul(dst, k_sum[:, u * 128:u * 128 + 128], q_st[:, u * 128:u * 128 + 128], start=True, stop=True)
                    else:
                        mm = PE.matmul(dst, K_c[:, u * 128:u * 128 + 128], comb(Qw, 1 << (term - 1), u), start=True, stop=True)
                mm.then_inc(lv_full, 1)

        def hg_turn_tensor(pe, i):
            pe.wait_ge(merged, i * LEVELS + LEVELS)
            for n in range(4):
                if n >= 2:
                    pe.wait_ge(kt_free, i * 4 + n - 1)
                d, half = divmod(n, 2)
                for u in range(4):
                    c = d * PC + (half * 4 + u) * 128
                    mm = PE.transpose(ps[:, KTB[n % 2], u * 128:u * 128 + 128], Kw[:, c:c + 128], ident)
                mm.then_inc(kt_full, 1)

        def hg_states_tensor(pe, i):
            pe.wait_ge(kt_free, i * 4 + 4)
            pe.wait_ge(moved, i + 1)
            pe.wait_ge(lv_free, i * 16 + 16)
            for s in range(3):
                for hd in range(2):
                    for d in range(2):
                        g = CHAIN[d][s]
                        mm = PE.matmul(ps[:, STB[s], (hd * 2 + d) * 128:(hd * 2 + d) * 128 + 128],
                                       kTw[:, 1 - d, hd * 4 + g, :], v_w[:, g, hd * 128:hd * 128 + 128], start=True, stop=True)
                mm.then_inc(st_full, 1)

        def hg_out_tensor(pe, i):
            pe.wait_ge(st_ready, i + 1)
            for hd in range(2):
                for g in range(4):
                    u = hd * 4 + g
                    dst = ps[:, OB[hd], g * 128:g * 128 + 128]
                    parts = [(v_w[:, g, hd * 128:hd * 128 + 128], A_w[:, u, :])]
                    if g:
                        parts.append((St[:, 1, hd, g - 1, :], Qw[:, PC + u * 128:PC + u * 128 + 128]))
                    back = {0: 0, 3: 1, 2: 2}.get(g)
                    if back is not None:
                        parts.append((St[:, 0, hd, back, :], Qw[:, u * 128:u * 128 + 128]))
                    for n, (a, b) in enumerate(parts):
                        mm = PE.matmul(dst, a, b, start=n == 0, stop=n == len(parts) - 1)
                mm.then_inc(o_full, 1)

        def hg_mean_tensor(pe, i):
            for hd in range(2):
                pe.wait_ge(o_squared, i * 2 + hd + 1)
                PE.matmul(ps[:, MSB[hd], :], ones[128], o_sq[:, hd, :], start=True, stop=True).then_inc(ms_full, 1)

        def hg_core_after(pe, i, idx):
            if idx == 0:
                hg_scores_tensor(pe, i, 0)
            if idx < 7:
                hg_scores_tensor(pe, i, idx + 1)
            if idx == 7:
                hg_turn_tensor(pe, i)
            if idx == 8:
                hg_states_tensor(pe, i)
            if idx == 9:
                hg_out_tensor(pe, i)
                hg_mean_tensor(pe, i)

        def outer_tensor(pe, name, src, n, kts, freed, freed_base, ready, done=()):
            def turn(t, reused):
                for j in range(4):
                    if reused or j >= len(done):
                        ring.wait_loaded(pe, name, j, t)
                    if reused:
                        pe.wait_ge(freed, (t - 1) * 4 + (freed_base + j + 1))
                    wj = strip(name, j, kts)
                    k0 = 0 if reused or j >= len(done) else done[j]
                    for k in range(k0, kts):
                        if not reused and j == 0:
                            ready(k)
                        mm = PE.matmul(ps[:, j, 0:n], wj[:, k, :], src(k), start=k == 0, stop=k == kts - 1)
                    strip_used(mm)
            turn(0, False)
            with pe.Fori(1, ring.stages[name]["turns"]) as t:
                turn(t, True)

        def wait_strip(eng, name, j, t):
            s = ring.stages[name]
            eng.wait_ge(strips_used, t * s["slots"] + (s["first"] + j + 1))

        def mla_in_tensor(pe):
            ring.wait_loaded(pe, "mla_a", 0, 0)
            wj = strip("mla_a", 0, 8)
            for m in range(2):
                for k in range(8):
                    if m == 0:
                        wait_h(pe, "mla_pre", k)
                    mm = PE.matmul(ps[:, 0, m * 256:m * 256 + 256], wj[:, k, m * 128:m * 128 + 128], hT[:, k, CTX:T],
                                   start=k == 0, stop=k == 7)
            strip_used(mm)
            ring.wait_loaded(pe, "mla_a", 1, 0)
            wj = strip("mla_a", 1, 8)
            for m in range(2):
                for k in range(8):
                    mm = PE.matmul(ps[:, 1 + m, :], wj[:, k, m * 128:m * 128 + 128], hT[:, k, :], start=k == 0, stop=k == 7)
            strip_used(mm)
            with pe.Fori(0, 2) as t:
                for j in range(4):
                    ring.wait_loaded(pe, "mla_z", j, t)
                    pe.wait_ge(z_kept, raised(t * 4 + max(j - 1, 0)))
                    wj = strip("mla_z", j, 8)
                    for m in range(2):
                        for k in range(8):
                            mm = PE.matmul(ps[:, 3 + j % 2, m * 256:m * 256 + 256], wj[:, k, m * 128:m * 128 + 128],
                                           hT[:, k, CTX:T], start=k == 0, stop=k == 7)
                    strip_used(mm)
            norm_tensor(pe, "qa", lambda k: sqm[:, k * LAT:k * LAT + LAT], ones[256], LAT)
            norm_tensor(pe, "kva", lambda k: sqm[:, 2 * LAT:2 * LAT + T], ones[128], T)
            pe.wait_ge(in_dve_kept, 3)
            pe.wait_ge(tab_loaded, TAB_ALL)
            PE.matmul(ps[:, 5, 0:LAT], rotm, kpe[:, CTX:T], start=True, stop=True).then_inc(rot_full, 1)

        def mla_pairs_tensor(pe):
            pe.wait_ge(qj_ready, 1)
            with pe.Fori(0, PAIRS // 2) as t:
                for j in range(2):
                    p = t * 2 + j
                    ring.wait_loaded(pe, "mla_b", j, t)
                    wn = ring.slot("mla_b", j)[:, 0:512].rearrange("p (k h c) -> p k h c", k=2, h=2)
                    wr = ring.slot("mla_b", j)[:, 512:768].rearrange("p (k c) -> p k c", k=2)
                    wkv = ring.slot("mla_b", j)[:, 768:1280].rearrange("p (h c) -> p h c", h=2)
                    pe.wait_ge(pt_kept, raised(p * 4))
                    for hd in range(2):
                        for k in range(2):
                            mm = PE.matmul(ps[:, 4, hd * 256:hd * 256 + 256], wn[:, k, hd, :], qa[:, k, :],
                                           start=k == 0, stop=k == 1)
                    mm.then_inc(mp_full, 1)
                    for k in range(2):
                        mm = PE.matmul(ps[:, 5, 0:256], wr[:, k, :], qa[:, k, :], start=k == 0, stop=k == 1)
                    mm.then_inc(mp_full, 1)
                    for hd in range(2):
                        PE.matmul(ps[:, hd, :], wkv[:, hd, 0:128], kva, start=True, stop=True).then_inc(mp_full, 1)
                    for g in range(NG):
                        mm = PE.matmul(ps[:, 2 + g // 2, (g % 2) * 256:(g % 2) * 256 + 256], kva[:, g * 128:g * 128 + 128],
                                       wkv[:, :, 128:256], start=True, stop=True)
                        if g == 1:
                            mm.then_inc(mp_full, 1)
                    strip_used(mm)
                    pe.wait_ge(mp_dve_kept, p * 4 + 1)
                    PE.matmul(ps[:, 5, 256:512], rotm, qpe, start=True, stop=True).then_inc(rot_full, 1)
                    pe.wait_ge(mp_dve_kept, p * 4 + 4)
                    pe.wait_ge(mp_act_kept, p * 3 + 3)
                    for c in range(4):
                        hd, qg = divmod(c, 2)
                        PE.matmul(ps[:, c, :], qn[:, hd, qg * 128:qg * 128 + 128], kn[:, hd, :], start=True, stop=False)
                        PE.matmul(ps[:, c, :], qpe[hd * 64:hd * 64 + 64, qg * 128:qg * 128 + 128],
                                  kpe[hd * 64:hd * 64 + 64, :], start=False, stop=True).then_inc(s_full, 1)
                    for c in range(4):
                        pe.wait_ge(p_ready, p * 4 + c + 1)
                        if c >= 2:
                            pe.wait_ge(pt_kept, raised(p * 4 + c - 1))
                        for g in range(NG):
                            mm = PE.transpose(ps[:, 4 + c % 2, g * 128:g * 128 + 128], Pm[:, c, g * 128:g * 128 + 128], ident)
                        mm.then_inc(pt_full, 1)
                    pe.wait_ge(pv_kept, raised(p))
                    for hd in range(2):
                        pe.wait_ge(pt_kept, raised(p * 4 + 2 * hd + 2))
                        for g in range(NG):
                            mm = PE.matmul(ps[:, 6, hd * 256:hd * 256 + 256], vm[:, g, hd * 128:hd * 128 + 128],
                                           PTm[:, hd, g, :], start=g == 0, stop=g == NG - 1)
                    mm.then_inc(pv_full, 1)

        def base(l):
            return dict(combo=32 + 32 * l, pv=8 + 16 * l, rot=9 + 5 * l, qj=1 + 5 * l, pvk=8 + 4 * l,
                        full=5 * l, act=5 * l, dve=3 + 5 * l, br=12 * l, brd=6 * l, bract=4 * l)

        def in_tensor(pe, l):
            b = base(l)
            c0 = CTX * l
            n, groups = T - c0, range(2 * l, NG)
            name = f"in{l}"
            ring.wait_loaded(pe, name, 0, 0)
            wj = strip(name, 0, 8)
            for k in range(8):
                wait_h(pe, f"mix{l}", k)
                mm = PE.matmul(ps[:, 0, :], wj[:, k, 0:128], hT[:, k, :], start=k == 0, stop=k == 7)
            mm.then_inc(in_full, 1)
            for g in range(NG):
                for k in range(8):
                    mm = PE.matmul(ps[:, 1, g * 128:g * 128 + 128], hT[:, k, g * 128:g * 128 + 128], wj[:, k, 128:256],
                                   start=k == 0, stop=k == 7)
            strip_used(mm)
            ring.wait_loaded(pe, name, 1, 0)
            for j in range(4):
                if j == 2:
                    ring.wait_loaded(pe, name, 2, 0)
                wj = strip(name, 1 + j // 2, 8)
                for k in range(8):
                    mm = PE.matmul(ps[:, 2 + j, 0:n], wj[:, k, (j % 2) * 128:(j % 2) * 128 + 128], hT[:, k, c0:T],
                                   start=k == 0, stop=k == 7)
                if j % 2:
                    strip_used(mm)
                else:
                    mm.then_inc(in_full, 1)
            for s, first_bank in ((3, 6), (4, 0)):
                ring.wait_loaded(pe, name, s, 0)
                if s == 4:
                    pe.wait_ge(in_act_kept, b["act"] + 1)
                    pe.wait_ge(in_dve_kept, b["dve"] + 1)
                wj = strip(name, s, 8)
                for n_g, g in enumerate(groups):
                    for k in range(8):
                        mm = PE.matmul(ps[:, first_bank + n_g // 2, (n_g % 2) * 256:(n_g % 2) * 256 + 256],
                                       hT[:, k, g * 128:g * 128 + 128], wj[:, k, :], start=k == 0, stop=k == 7)
                    if n_g == 1 and l == 0:
                        mm.then_inc(in_full, 1)
                strip_used(mm)
            pe.wait_ge(in_act_kept, b["act"] + 2)
            PE.matmul(ps[:, 2, 0:LAT], rotb, kb[:, CTX:T], start=True, stop=True).then_inc(rot_full, 1)

        def side_turned(pe, j, n):
            pe.wait_ge(rows_kept, j * 6 + (mod_turn["mod1"] * 3 + n + 1))
            for m in range(2):
                PE.matmul(ps[:, 0, n * 4 + m * 2:n * 4 + m * 2 + 2], mod_rows[0:2, n % 2 * 512 + m * 128:n % 2 * 512 + m * 128 + 128],
                          ident[0:2, 0:2], start=True, stop=True).then_inc(mod_turned, 1)

        def side_tensor(pe, j, n):
            if n:
                side_turned(pe, j, n - 1)
            ring.wait_loaded(pe, "mod1", n, j)
            wj = strip("mod1", n, 8)
            for k in range(8):
                mm = PE.matmul(ps[0:2, 0, 256:512], view(sil, (8, 2), at=16 + k), wj[:, k, :], start=k == 0, stop=k == 7)
            strip_used(mm)

        SIDE_OF = ((0, 1), (2, None), (3, 4), (5, None))

        def attend_tensor(pe, l):
            b = base(l)
            groups = range(2 * l, NG)
            nc_, nseq = 2 * len(groups), 2 - l
            combos = [(h2, g) for h2 in range(2) for g in groups]
            pe.wait_ge(in_act_kept, b["act"] + 5)
            pe.wait_ge(in_dve_kept, b["dve"] + 5 - 2 * l)
            pe.wait_ge(qj_ready, b["qj"] + 1)
            with pe.Fori(0, 4) as j:
                if l == 0:
                    pe.wait_ge(mod_ready, j + 3)
                PE.matmul(ps[:, 0, 0:LAT], rotb, q_raw[:, j, LAT * (1 - l):LAT * (1 - l) + LAT], start=True, stop=True).then_inc(rot_full, 1)
                pe.wait_ge(qj_ready, j + (b["qj"] + 2))

                def scores(c):
                    h2, g = combos[c]
                    nk = CTX if g < 2 else T
                    if c >= 4:
                        pe.wait_ge(s_max, j * nc_ + (b["combo"] + c - 3))
                    PE.matmul(ps[:, 2 + c % 4, 0:nk], qj[h2 * 64:h2 * 64 + 64, g * 128:g * 128 + 128], kb[h2 * 64:h2 * 64 + 64, 0:nk],
                              start=True, stop=True).then_inc(s_full, 1)

                scores(0)
                scores(1)
                for s in range(nc_ // 2):
                    if 2 * s + 2 < nc_:
                        scores(2 * s + 2)
                        scores(2 * s + 3)
                    if l == 0:
                        side_tensor(pe, j, SIDE_OF[s][0])
                    for c in (2 * s, 2 * s + 1):
                        h2, g = combos[c]
                        kgs = 2 if g < 2 else 4
                        pe.wait_ge(p_ready, j * nc_ + (b["combo"] + c + 1))
                        pe.wait_ge(pt_kept, raised(j * nc_ + (b["combo"] + c - 1)))
                        for kg in range(kgs):
                            mm = PE.transpose(ps[:, (6, 1)[c % 2], kg * 128:kg * 128 + 128],
                                              sc[:, c % 4, kg * 128:kg * 128 + 128], ident)
                        mm.then_inc(pt_full, 1)
                    if l == 0 and SIDE_OF[s][1] is not None:
                        side_tensor(pe, j, SIDE_OF[s][1])
                    if s == 0:
                        pe.wait_ge(pv_kept, raised(j + b["pvk"]))
                    pe.wait_ge(pt_kept, raised(j * nc_ + (b["combo"] + 2 * s + 2)))
                    g0 = g - g % 2
                    for kg in range(kgs):
                        mm = PE.matmul(ps[h2 * 64:h2 * 64 + 64, 7, g0 * 128:g0 * 128 + 256], vb[:, kg, h2 * 64:h2 * 64 + 64],
                                       PTb[:, kg, :], start=kg == 0, stop=kg == kgs - 1)
                    mm.then_inc(pv_full, 1)
                if l == 0:
                    side_turned(pe, j, 5)
            if l == 0:
                pe.wait_ge(mod_ready, 7)

        def branches_tensor(pe, l):
            b = base(l)
            seqs = range(l, 2)
            pe.wait_ge(pv_kept, raised(b["pvk"] + 4))
            for gp in range(2):
                for s in seqs:
                    for e in range(2):
                        for st in range(2):
                            mm = PE.matmul(ps[e * 64:e * 64 + 64, gp, s * 256:s * 256 + 256],
                                           ub[:, 2 * s + st, (2 * gp + e) * 64:(2 * gp + e) * 64 + 64], poolm[:, st, 2 * gp + e, :],
                                           start=st == 0, stop=st == 1)
                mm.then_inc(br_full, 1)
            n = 0
            for ct in range(2):
                for s in seqs:
                    bank = 2 + n
                    for st in range(2):
                        mm = PE.matmul(ps[:, bank, :], fb[:, 2 * s + st, ct * 128:ct * 128 + 128], dftm[:, st, :],
                                       start=st == 0, stop=st == 1)
                    mm.then_inc(br_full, 1)
                    n += 1
            for gp in range(2):
                pe.wait_ge(br_dve_kept, b["brd"] + gp + 1)
                PE.matmul(ps[:, gp, l * 256:512], poolw[:, l, gp, :], pooled[:, gp, l * 256:512], start=True, stop=True).then_inc(br_full, 1)
            n = 0
            for ct in range(2):
                for s in seqs:
                    pe.wait_ge(br_dve_kept, b["brd"] + 3 + n)
                    PE.matmul(ps[:, 6, s * 256:s * 256 + 256] if ct == 0 else ps[:, 7, s * 256:s * 256 + 256], dftc[:, 0, :],
                              fcs[:, n % 2, 0:256], start=True, stop=False)
                    mm = PE.matmul(ps[:, 6, s * 256:s * 256 + 256] if ct == 0 else ps[:, 7, s * 256:s * 256 + 256], dftc[:, 1, :],
                                   fcs[:, n % 2, 256:512], start=False, stop=True)
                    mm.then_inc(br_full, 1)
                    n += 1

        def merge_tensor(pe, l):
            b = base(l)
            n, c0 = T - CTX * l, CTX * l
            name = f"merge{l}"
            pe.wait_ge(br_act_kept, b["bract"] + 4)
            with pe.Fori(0, 4) as t:
                for m in range(2):
                    for j in range(3):
                        if m == 0:
                            ring.wait_loaded(pe, name, j, t)
                        if j == 0:
                            pe.wait_ge(gates_ready, raised(t * 6 + (3 * m + 24 * l)))
                        wj = strip(name, j, 8)
                        for k in range(8):
                            mm = PE.matmul(ps[:, j, 0:n], wj[:, k, m * 128:m * 128 + 128], hT[:, k, c0:T], start=k == 0, stop=k == 7)
                        if m == 0:
                            mm.then_inc(mg_full, 1)
                        else:
                            strip_used(mm)
                    if m == 0:
                        ring.wait_loaded(pe, name, 3, t)
                    pe.wait_ge(mg_read, raised(t * 2 + (m + 8 * l)))
                    wj = strip(name, 3, 8)
                    for j, (k0, k1) in enumerate(((0, 4), (4, 6), (6, 8))):
                        for k in range(k0, k1):
                            mm = PE.matmul(ps[:, 3 + j, 0:n], wj[:, k, m * 128:m * 128 + 128], brT[:, k, c0:T],
                                           start=k == k0, stop=k == k1 - 1)
                        if j < 2 or m == 0:
                            mm.then_inc(mg_full, 1)
                strip_used(mm)

        def wait_merge(eng, l, t, m, bank):
            if m == 1 and bank in (0, 1, 2, 5):
                wait_strip(eng, f"merge{l}", min(bank, 3), t)
            else:
                eng.wait_ge(mg_full, t * 8 + (32 * l + (4 if m else 1) + bank))

        def out_tensor(pe, l):
            n, c0 = T - CTX * l, CTX * l
            pe.wait_ge(gates_ready, raised(24 * l + 24))
            for j in range(4):
                ring.wait_loaded(pe, f"out{l}", j, 0)
                wj = strip(f"out{l}", j, 8)
                for m in range(2):
                    for k in range(8):
                        if j == 0 and m == 0:
                            pe.wait_ge(y_ready, raised(8 * l + k + 1))
                        mm = PE.matmul(ps[:, 2 * j + m, 0:n], wj[:, k, m * 128:m * 128 + 128], yT[:, k, c0:T],
                                       start=k == 0, stop=k == 7)
                    if m == 0:
                        mm.then_inc(out_full, 1)
                strip_used(mm)

        def up_tensor(pe, l):
            n, c0 = T - CTX * l, CTX * l
            name = f"up{l}"

            def turn(t, reused):
                for j in range(2):
                    ring.wait_loaded(pe, name, j, t)
                    if reused:
                        pe.wait_ge(conv_ready, t * 2 + (j - 1 + FT * l))
                    wj = strip(name, j, 8)
                    for m in range(2):
                        for k in range(8):
                            if not reused and j == 0 and m == 0:
                                wait_h(pe, f"ffn{l}", k)
                            mm = PE.matmul(ps[:, 2 * j + m, 0:n], wj[:, k, m * 128:m * 128 + 128], hT[:, k, c0:T],
                                           start=k == 0, stop=k == 7)
                    strip_used(mm)
            turn(0, False)
            with pe.Fori(1, FT // 2) as t:
                turn(t, True)

        XB = dict(hg_out=0, mla_out=8, out0=16, down0=24, out1=32, down1=40)

        @block.tensor
        def _(pe):
            pe.wait_ge(tab_loaded, 16)
            pe.wait_ge(x_loaded, 32)
            for k in range(KT):
                if k >= 4:
                    pe.wait_ge(x_copied, k - 3)
                for g in range(NG):
                    mm = PE.transpose(ps[:, k % 4, g * 128:g * 128 + 128], x_in[:, g, k * 128:k * 128 + 128], ident)
                mm.then_inc(x_turned, 1)
            pe.wait_ge(vec_loaded, 16 * N_VEC)
            at_ = 0
            for n, rows in enumerate(VROWS):
                bank, col = (6, at_) if n < 5 else (7, 0)
                mm = PE.transpose(ps[:, bank, col:col + rows], v_in[n][0:rows, :], ident[0:rows, 0:rows])
                at_ += rows
            mm.then_inc(vec_turned, 1)
            pe.wait_ge(sil_ready, 1)
            pe.wait_ge(x_copied, KT)
            mods_tensor(pe, "ada0", 0, 0, 1)
            norm_tensor(pe, "hg_pre", lambda k: hT[:, k, :], ones[1024], T)
            mods_tensor(pe, "ada0", 0, 1, 2)
            for idx in range(10):
                hg_project_tensor(pe, 0, idx)
            with pe.Fori(1, PAIRS) as i:
                for idx in range(10):
                    hg_project_tensor(pe, i, idx)
                    hg_core_after(pe, i - 1, idx)
            pe.wait_ge(act_freed, PAIRS * 6)
            EARLY = HG_HEADS - 2
            early = [(j, k) for j in range(2) for k in range(EARLY)]
            for idx in range(10):
                hg_core_after(pe, PAIRS - 1, idx)
                for j, k in early[4 * idx:4 * idx + 4]:
                    if k == 0:
                        ring.wait_loaded(pe, "hg_out", j, 0)
                    if j == 0 and k == 0:
                        pe.wait_ge(o_ready, raised(EARLY))
                    PE.matmul(ps[:, j, :], strip("hg_out", j, 16)[:, k, :], oz[:, k, :], start=k == 0, stop=False)

            def o_heads(k):
                if k >= EARLY:
                    pe.wait_ge(o_ready, raised(k + 1))
            outer_tensor(pe, "hg_out", lambda k: oz[:, k, :], T, 16, y_kept, 0, o_heads, (EARLY, EARLY))
            norm_tensor(pe, "hg_post", lambda k: oz[:, k, :], ones[1024], T)
            pe.wait_ge(mod_ready, 1)
            mods_tensor(pe, "ada1", 0, 0, 1)
            norm_tensor(pe, "mla_pre", lambda k: hT[:, k, :], ones[1024], T)
            mods_tensor(pe, "ada1", 0, 1, 2)
            mla_in_tensor(pe)
            mla_pairs_tensor(pe)
            pe.wait_ge(pv_kept, raised(8))
            pe.wait_ge(ctx2_loaded, 16)
            for k in range(KT):
                for g in range(2):
                    mm = PE.transpose(ps[:, 4 + k // 2, (k % 2) * 256 + g * 128:(k % 2) * 256 + g * 128 + 128],
                                      ctx2_in[:, g, k * 128:k * 128 + 128], ident)
                if k % 2:
                    mm.then_inc(x_turned, 1)
            outer_tensor(pe, "mla_out", lambda k: ozm[:, k, :], LAT, 16, y_kept, 8, lambda k: None)
            pe.wait_ge(x_copied, KT + 4)
            norm_tensor(pe, "mla_post", lambda k: ozm[:, k, :], ones[1024], LAT)
            for l in range(2):
                n, c0 = T - CTX * l, CTX * l
                if l == 0:
                    pe.wait_ge(mod_ready, 2)
                    mods_tensor(pe, "mod0", 16, 0, 1)
                norm_tensor(pe, f"mix{l}", lambda k: hT[:, k, :], ones[1024], T)
                if l == 0:
                    mods_tensor(pe, "mod0", 16, 1, 4)
                in_tensor(pe, l)
                attend_tensor(pe, l)
                branches_tensor(pe, l)
                merge_tensor(pe, l)
                out_tensor(pe, l)
                norm_tensor(pe, f"ffn{l}", lambda k: hT[:, k, 0:n], ones[1024], n)
                up_tensor(pe, l)
                pe.wait_ge(conv_ready, FT * (l + 1))
                outer_tensor(pe, f"down{l}", lambda k: hid[:, k, 0:n], n, FT, x_added, XB[f"down{l}"],
                             lambda k: pe.wait_ge(hid_ready, raised(FT * l + k + 1)))
            norm_tensor(pe, "final", lambda k: hT[:, k, 0:LAT], ones[1024], LAT)
            pe.wait_ge(h_ready, FINAL_READY)
            for k in range(KT):
                for g in range(2):
                    mm = PE.transpose(ps[:, k // 2, (k % 2) * 256 + g * 128:(k % 2) * 256 + g * 128 + 128],
                                      hT[:, k, g * 128:g * 128 + 128], ident)
                if k % 2:
                    mm.then_inc(o_turned, 1)

        def hg_project_scalar(act, i, idx):
            wait_projected(act, i, idx)
            bank = ps[:, idx % 2, :]
            m = idx % 2
            first_turn = isinstance(i, int) and i == 0
            if idx < 4:
                d = 1 - idx // 2
                if idx == 0 and not first_turn:
                    act.wait_ge(unpacked, i)
                    act.wait_ge(moved, i)
                S.activation(f_st[:, d, m * T:m * T + T], bank, ACT.Sigmoid)
                S.activation(k_st[:, d, m * T:m * T + T], bank, ACT.Sigmoid, scale=-1.0).then_inc(act_freed, 1)
            elif idx < 8:
                if idx >= 6:
                    act.wait_ge(dve_freed, i * 4 + idx - 5)
                elif idx == 4 and not first_turn:
                    act.wait_ge(o_ready, raised(i * 2 - 2))
                S.activation(sg[:, m, :], bank, ACT.Sigmoid).then_inc(sig_ready, 1)
            else:
                S.activation(v_st[:, 2 * m:2 * m + 2, :], bank, ACT.Copy).then_inc(act_freed, 1)

        def hg_keys_scalar(act, i, term):
            if term == 1:
                act.wait_ge(unpacked, i + 1)
            else:
                act.wait_ge(merged, i * LEVELS + term - 1)
            h = 1 << (term - 1)
            S.activation(view(K_c, (2 * h, PC // (2 * h)), (h, 2), (1, h)), comb(Kw, h), ACT.Copy).then_inc(kc_ready, 1)

        def hg_turn_scalar(act, i):
            for n in range(4):
                act.wait_ge(kt_full, i * 4 + n + 1)
                d, half = divmod(n, 2)
                S.activation(kTw[:, d, half * 4:half * 4 + 4, :], ps[:, KTB[n % 2], :], ACT.Copy).then_inc(kt_free, 1)

        def hg_mean_scalar(act, i):
            for hd in range(2):
                act.wait_ge(o_full, raised(i * 2 + hd + 1))
                S.activation(o_sq[:, hd, :], ps[:, OB[hd], :], ACT.Square).then_inc(o_squared, 1)
            for hd in range(2):
                act.wait_ge(ms_full, i * 2 + hd + 1)
                S.activation(hg_root[hd], ps[:, MSB[hd], :], ACT.Sqrt, bias=eps).then_inc(rt_ready, 1)

        hg_root = (root, rstd)

        def y_scalar(act, name, n, base_):
            with act.Fori(0, 2) as t:
                for j in range(4):
                    wait_strip(act, name, j, t)
                    S.activation(view(hT, (1, n), at=t * (4 * T) + j * T), ps[:, j, 0:n], ACT.Copy).then_inc(y_kept, 1)

        def mla_scalar(act):
            with act.Fori(0, 2) as t:
                for j in range(4):
                    wait_strip(act, "mla_z", j, t)
                    act.wait_ge(z_kept, raised(t * 4 + max(j - 1, 0)))
                    S.activation(sgm[:, j % 2, :], ps[:, 3 + j % 2, :], ACT.Sigmoid).then_inc(z_signed, 1)
            act.wait_ge(in_dve_kept, 2)
            norm_scalar(act, "qa", lambda k: qa[:, k, :], lambda k: sqm[:, k * LAT:k * LAT + LAT], LAT)
            norm_scalar(act, "kva", lambda k: kva, lambda k: sqm[:, 2 * LAT:2 * LAT + T], T)
            with act.Fori(0, PAIRS // 2) as t:
                for j in range(2):
                    p = t * 2 + j
                    act.wait_ge(mp_full, p * 5 + 1)
                    S.activation(qn.rearrange("p h t -> p (h t)"), ps[:, 4, :], ACT.Copy).then_inc(mp_act_kept, 1)
                    for hd in range(2):
                        act.wait_ge(mp_full, p * 5 + 3 + hd)
                        S.activation(kn[:, hd, :], ps[:, hd, :], ACT.Copy).then_inc(mp_act_kept, 1)
                    for c in range(4):
                        act.wait_ge(s_max, p * 4 + c + 1)
                        S.activation(Pm[:, c, :], ps[:, c, :], ACT.Exp, scale=MLA_SCALE, bias=stm[:, c, 1:2],
                                     accum_out=stm[:, c, 2:3]).then_inc(s_exp, 1)
                    for c in range(4):
                        hd, qg = divmod(c, 2)
                        act.wait_ge(pt_full, p * 4 + c + 1)
                        S.activation(PTm[:, hd, :, qg * 128:qg * 128 + 128],
                                     ps[:, 4 + c % 2, :].rearrange("p (g q) -> p g q", g=NG), ACT.Copy).then_inc(pt_kept, 1)

        def in_scalar(act, l):
            b = base(l)
            c0 = CTX * l
            act.wait_ge(in_full, b["full"] + 1)
            S.activation(kb, ps[:, 0, :], ACT.Copy).then_inc(in_act_kept, 1)
            for j in range(4):
                if j % 2:
                    wait_strip(act, f"in{l}", 1 + j // 2, 0)
                else:
                    act.wait_ge(in_full, b["full"] + 2 + j // 2)
                S.activation(q_raw[:, j, 0:T - c0], ps[:, 2 + j, 0:T - c0], ACT.Copy).then_inc(in_act_kept, 1)

        def attend_scalar(act, l):
            b = base(l)
            groups = range(2 * l, NG)
            nc_ = 2 * len(groups)
            combos = [(h2, g) for h2 in range(2) for g in groups]
            with act.Fori(0, 4) as j:
                def exp(c):
                    nk = CTX if combos[c][1] < 2 else T
                    h2 = combos[c][0]
                    act.wait_ge(s_max, j * nc_ + (b["combo"] + c + 1))
                    S.activation(sc[:, c % 4, 0:nk], sc[:, c % 4, 0:nk], ACT.Exp, bias=stb[:, c % 4, 1:2],
                                 accum_out=stb[:, c % 4, 2:3])
                    S.activation(stb[:, c % 4, 3:4], sink[:, bass.ds(j + (l * 8 + h2 * 4), 1)], ACT.Exp,
                                 bias=stb[:, c % 4, 1:2]).then_inc(s_exp, 1)

                def keep(c):
                    h2, g = combos[c]
                    kgs = 2 if g < 2 else 4
                    act.wait_ge(pt_full, j * nc_ + (b["combo"] + c + 1))
                    if c % 2 == 0:
                        act.wait_ge(pv_full, j * (nc_ // 2) + (b["pv"] + c // 2))
                    S.activation(PTb[:, 0:kgs, (g % 2) * 128:(g % 2) * 128 + 128],
                                 ps[:, (6, 1)[c % 2], 0:kgs * 128].rearrange("p (g q) -> p g q", g=kgs), ACT.Copy).then_inc(pt_kept, 1)

                def side(n):
                    wait_strip(act, "mod1", n, j)
                    S.activation(mod_rows[0:2, n % 2 * 512:n % 2 * 512 + 256], ps[0:2, 0, 256:512], ACT.Copy).then_inc(rows_kept, 1)

                exp(0)
                exp(1)
                for s in range(nc_ // 2):
                    if 2 * s + 2 < nc_:
                        exp(2 * s + 2)
                        exp(2 * s + 3)
                    if l == 0:
                        side(SIDE_OF[s][0])
                    keep(2 * s)
                    keep(2 * s + 1)
                    if l == 0 and SIDE_OF[s][1] is not None:
                        side(SIDE_OF[s][1])
                act.wait_ge(pv_full, j * (nc_ // 2) + (b["pv"] + nc_ // 2))
                S.activation(view(brT, (1, T - CTX * l), at=j * T + CTX * l), ps[:, 7, CTX * l:T], ACT.Copy).then_inc(pv_kept, 1)

        def branches_scalar(act, l):
            b = base(l)
            ns = 2 - l
            for gp in range(2):
                act.wait_ge(br_full, b["br"] + 2 + 2 * ns + gp + 1)
                S.activation(brT[:, 4 + gp, l * 256:T], ps[:, gp, l * 256:T], ACT.Identity,
                             scale=vecs[:, PSC + 2 * l + gp:PSC + 2 * l + gp + 1]).then_inc(br_act_kept, 1)
            for ct in range(2):
                act.wait_ge(br_full, b["br"] + 4 + 2 * ns + ns * (ct + 1))
                S.activation(brT[:, 6 + ct, l * 256:T], ps[:, 6 + ct, l * 256:T], ACT.Copy).then_inc(br_act_kept, 1)

        def merge_scalar(act, l):
            n = T - CTX * l
            with act.Fori(0, 4) as t:
                for m in range(2):
                    act.wait_ge(mg_read, raised(t * 2 + (m + 8 * l)))
                    for j in range(3):
                        wait_merge(act, l, t, m, j)
                        S.activation(gts[:, j, 0:n], ps[:, j, 0:n], ACT.Sigmoid).then_inc(gates_ready, 1)

        def up_scalar(act, l):
            n = T - CTX * l
            def tap(k, f, part):
                return vecs[:, bass.ds(f + (CONV + (l * 3 + k) * 44 + part * FT), 1)]
            with act.Fori(0, FT // 2) as t:
                for j in range(2):
                    f = t * 2 + j
                    wait_strip(act, f"up{l}", j, t)
                    if j == 0:
                        act.wait_ge(hid_ready, raised(f + FT * l))
                    for part in range(2):
                        S.activation(acc[:, 2 * j + part, 0:n], ps[:, 2 * j + part, 0:n], ACT.Identity,
                                     scale=tap(1, f, part)).then_inc(tap_ready, 1)
                for j in range(2):
                    f = t * 2 + j
                    act.wait_ge(conv_ready, f + (FT * l + 1))
                    S.activation(sgf[:, j, 0:n], acc[:, 2 * j + 1, 0:n], ACT.Sigmoid).then_inc(sf_ready, 1)

        @block.scalar
        def _(act):
            for rows, src in VSRC[0::2]:
                tile_, r0, r1 = rows
                act.dma_start(v_in[tile_][r0:r1, :], src).then_inc(vec_loaded, 16)
            act.dma_start(sink, bass.AP(w["attn_sink_2"].tensor, 0, [[0, 128], [1, 16]])).then_inc(vec_loaded, 16)
            def conditions():
                act.wait_ge(vec_ready, 1)
                S.activation(sil, vecs[:, 0:32], ACT.Sigmoid).then_inc(sig_c, 1)
                rows_scalar(act, "ada0", 0, 1)

            xcol = lambda k: xT[:, k, :]
            act.wait_ge(x_copied, KT)
            norm_scalar(act, "hg_pre", xcol, lambda k: hT[:, k, :], T, conditions)
            rows_scalar(act, "ada0", 1, 2)
            modulate_scalar(act, "hg_pre", mod_a[0], (0, 1))
            act.wait_ge(vec_loaded, 16 * N_VEC)
            for idx in range(10):
                hg_project_scalar(act, 0, idx)
            with act.Fori(1, PAIRS) as i:
                for idx in range(10):
                    if idx < LEVELS:
                        hg_keys_scalar(act, i - 1, idx + 1)
                    hg_project_scalar(act, i, idx)
                    if idx == 7:
                        hg_turn_scalar(act, i - 1)
                hg_mean_scalar(act, i - 1)
            for term in range(1, LEVELS + 1):
                hg_keys_scalar(act, PAIRS - 1, term)
            hg_turn_scalar(act, PAIRS - 1)
            hg_mean_scalar(act, PAIRS - 1)
            y_scalar(act, "hg_out", T, 0)
            act.wait_ge(y_kept, 8)
            norm_scalar(act, "hg_post", lambda k: hT[:, k, :], lambda k: oz[:, k, :], T)
            rows_scalar(act, "ada1", 0, 1)
            act.wait_ge(x_added, 8)
            norm_scalar(act, "mla_pre", xcol, lambda k: hT[:, k, :], T)
            rows_scalar(act, "ada1", 1, 2)
            modulate_scalar(act, "mla_pre", mod_a[1], (0, 1))
            mla_scalar(act)
            y_scalar(act, "mla_out", LAT, 8)
            act.wait_ge(y_kept, 16)
            norm_scalar(act, "mla_post", lambda k: hT[:, k, 0:LAT], lambda k: ozm[:, k, :], LAT)
            for l in range(2):
                n, c0 = T - CTX * l, CTX * l
                if l == 0:
                    rows_scalar(act, "mod0", 0, 1)
                act.wait_ge(x_added, 16 + 16 * l)
                act.wait_ge(x_copied, KT + 4)
                norm_scalar(act, f"mix{l}", xcol, lambda k: hT[:, k, :], T)
                if l == 0:
                    rows_scalar(act, "mod0", 1, 4)
                modulate_scalar(act, f"mix{l}", mod_b[l][:, 0:8, :], (0, 1))
                in_scalar(act, l)
                attend_scalar(act, l)
                branches_scalar(act, l)
                merge_scalar(act, l)
                act.wait_ge(x_added, 24 + 16 * l)
                norm_scalar(act, f"ffn{l}", lambda k: xT[:, k, c0:T], lambda k: hT[:, k, 0:n], n)
                modulate_scalar(act, f"ffn{l}", mod_b[l][:, 24:32, :], range(l, 2))
                up_scalar(act, l)
            act.wait_ge(x_added, 48)
            norm_scalar(act, "final", lambda k: xT[:, k, CTX:T], lambda k: hT[:, k, 0:LAT], LAT)
            for k in range(8):
                act.wait_ge(normed, sq_base["final"] + k + 1)
                S.activation(hT[:, k, 0:LAT], hT[:, k, 0:LAT], ACT.Identity, scale=vecs[:, FINAL + k:FINAL + k + 1]).then_inc(h_ready, 1)

        def hg_unpack_vector(dve, st, i):
            first = isinstance(i, int) and i == 0
            if not first:
                dve.wait_ge(o_full, raised(i * 2))
            dve.wait_ge(act_freed, i * 6 + 4)
            dve.wait_ge(dve_freed, i * 4 + 2)
            V.tensor_tensor(view(Qw, (PC, 2), (1, PC)), view(q_st, (0, 2), (1, PC)), f_st, ALU.mult)
            V.tensor_copy(Kw[:, 0:PC], k_st[:, 1, :])
            V.tensor_copy(Kw[:, PC:2 * PC], k_st[:, 0, :])
            if not first:
                dve.wait_ge(ms_full, i * 2)
            V.tensor_tensor(k_sum, k_st[:, 0, :], k_st[:, 1, :], ALU.add).then_inc(unpacked, 1)

        def hg_scores_vector(dve, st, i, term):
            src = [ps[:, LV[b], :].rearrange("p (u t) -> p u t", u=4) for b in range(2)]
            dst = [A_w[:, 4 * b:4 * b + 4, :] for b in range(2)]
            if term == 0:
                for b in range(2):
                    dve.wait_ge(lv_full, i * 16 + b + 1)
                    V.tensor_copy(dst[b], src[b]).then_inc(lv_free, 1)
                return
            h = 1 << (term - 1)
            n = PC // (2 * h)
            if term == 1:
                dve.wait_ge(moved, i + 1)
            dve.wait_ge(kc_ready, i * LEVELS + term)
            V.tensor_tensor(comb(Kw, h), comb(Kw, h), view(Tw, (2 * h, n), (-PC - h, 2), (0, h), at=PC + h), ALU.mult)
            dve.wait_ge(lv_full, i * 16 + 2 * term + 2)
            V.tensor_tensor(comb(Qw, h), comb(Qw, h), view(Tw, (2 * h, n), (PC - h, 2), (0, h), at=h), ALU.mult).then_inc(merged, 1)
            for b in range(2):
                mask = view(masks_i, (0, 4), (1, 128), at=(term - 1) * 128)
                V.copy_predicated(dst[b], mask, src[b]).then_inc(lv_free, 1)
            dve.wait_ge(merged, i * LEVELS + term)
            st.link(V.tensor_tensor(view(Tw, (PC, 2), (2 * h, n)), view(Tw, (PC, 2), (2 * h, n)),
                                    view(Tw, (PC, 2), (2 * h, n), at=h), ALU.mult))

        def hg_states_vector(dve, st, i):
            for s in range(3):
                dve.wait_ge(st_full, i * 3 + s + 1)
                for hd in range(2):
                    for d in range(2):
                        src = ps[:, STB[s], (hd * 2 + d) * 128:(hd * 2 + d) * 128 + 128]
                        dst = St[:, d, hd, s, :]
                        if s == 0:
                            ins = V.tensor_copy(dst, src)
                        else:
                            tot = Tw[:, d * PC + (hd * 4 + CHAIN[d][s]) * 128:][:, 0:1]
                            ins = V.scalar_tensor_tensor(dst, St[:, d, hd, s - 1, :], tot, src, ALU.mult, ALU.add)
                if s < 2:
                    st.link(ins)
                else:
                    ins.then_inc(st_ready, 1)

        def hg_gate_vector(dve, i, idx):
            m = idx % 2
            first_turn = isinstance(i, int) and i == 0
            dve.wait_ge(sig_ready, i * 4 + idx - 3)
            bank = ps[:, idx % 2, :]
            if idx < 6:
                if idx == 4 and not first_turn:
                    dve.wait_ge(lv_full, i * 16 - 14)
                V.tensor_tensor(q_st[:, m * T:m * T + T], bank, sg[:, m, :], ALU.mult).then_inc(dve_freed, 1)
            else:
                V.tensor_tensor(view(oz, (1, T), at=(i * 2 + m) * T), bank, sg[:, m, :], ALU.mult).then_inc(dve_freed, 1)

        def hg_read_vector(dve, st, i):
            for hd in range(2):
                dve.wait_ge(rt_ready, raised(i * 2 + hd + 1))
                zs = view(oz, (1, T), at=(i * 2 + hd) * T)
                V.reciprocal(hg_root[hd], hg_root[hd])
                st.link(V.tensor_tensor(o_tmp[:, hd, :], ps[:, OB[hd], :], zs, ALU.mult))
                V.scalar_tensor_tensor(zs, o_tmp[:, hd, :], vecs[:, OG:OG + 1], hg_root[hd], ALU.mult, ALU.mult).then_inc(o_ready, 1)

        def post_vector(dve, st, name, gate, gain, c0, n):
            st.link(V.tensor_tensor(coef, gate, view(gain, (1, 8), (0, 2)), ALU.mult))
            norm_vector(dve, st, name, n)
            for k in range(8):
                V.tensor_tensor(hT[:, k, 0:n], hT[:, k, 0:n], rstd[:, 0:n], ALU.mult).then_inc(normed, 1)
            for k in range(8):
                dve.wait_ge(normed, sq_base[name] + k + 1)
                for s in range(n // 256):
                    c = s + c0 // 256
                    cols = slice(c0 + s * 256, c0 + s * 256 + 256)
                    ins = V.scalar_tensor_tensor(xT[:, k, cols], hT[:, k, s * 256:s * 256 + 256], coef[:, k, c:c + 1],
                                                 xT[:, k, cols], ALU.mult, ALU.add)
                ins.then_inc(x_added, 1)

        def mod_vector(dve, name, turns, dst, bias):
            dve.wait_ge(mod_turned, (mod_turn[name] + turns) * 12)
            m = turns * 12
            V.tensor_tensor(dst, ps[:, 6, 0:2 * m].rearrange("p (m c) -> p m c", c=2), view(vecs, (1, m), (0, 2), at=bias),
                            ALU.add).then_inc(mod_ready, 1)

        def rope_vector(st, dst, raw, rot, cos, sin, tmp):
            V.tensor_tensor(tmp, rot, sin, ALU.mult)
            st.link(V.tensor_tensor(dst, raw, cos, ALU.mult))
            return V.tensor_tensor(dst, dst, tmp, ALU.add)

        def mla_vector(dve, st):
            wait_strip(dve, "mla_a", 0, 0)
            V.tensor_copy(qa.rearrange("p k t -> p (k t)"), ps[:, 0, :]).then_inc(in_dve_kept, 1)
            wait_strip(dve, "mla_a", 1, 0)
            V.tensor_copy(kva, ps[:, 1, :]).then_inc(in_dve_kept, 1)
            V.tensor_copy(kpe, ps[:, 2, :]).then_inc(in_dve_kept, 1)
            with dve.Fori(0, 2) as t:
                for j in range(4):
                    dve.wait_ge(z_signed, t * 4 + j + 1)
                    V.tensor_tensor(view(ozm, (1, T), at=(t * 8 + j * 2) * LAT), ps[:, 3 + j % 2, :], sgm[:, j % 2, :],
                                    ALU.mult).then_inc(z_kept, 1)
            norm_vector(dve, st, "qa", LAT)
            for k in range(2):
                V.scalar_tensor_tensor(qa[:, k, :], qa[:, k, :], vecs[:, QAG + k:QAG + k + 1], rstd[:, 0:LAT],
                                       ALU.mult, ALU.mult).then_inc(normed, 1)
            norm_vector(dve, st, "kva", T)
            V.scalar_tensor_tensor(kva, kva, vecs[:, KVG:KVG + 1], rstd, ALU.mult, ALU.mult).then_inc(normed, 1)
            dve.wait_ge(tab_loaded, TAB_ALL)
            dve.wait_ge(rot_full, 1)
            rope_vector(st, kpe[:, CTX:T], kpe[:, CTX:T], ps[:, 5, 0:LAT], cosm, sinm, krot).then_inc(qj_ready, 1)
            with st.loop(0, PAIRS // 2, 2 * 9) as t:
                for j in range(2):
                    p = t * 2 + j
                    dve.wait_ge(mp_full, p * 5 + 2)
                    V.tensor_copy(qpe, ps[:, 5, 0:256]).then_inc(mp_dve_kept, 1)
                    dve.wait_ge(mp_full, p * 5 + 5)
                    V.tensor_copy(vm[:, 0:2, :], ps[:, 2, :]).then_inc(mp_dve_kept, 1)
                    wait_strip(dve, "mla_b", j, t)
                    V.tensor_copy(vm[:, 2:4, :], ps[:, 3, :]).then_inc(mp_dve_kept, 1)
                    dve.wait_ge(rot_full, p + 2)
                    rope_vector(st, qpe, qpe, ps[:, 5, 256:512], cosm, sinm, qrot).then_inc(mp_dve_kept, 1)
                    for c in range(4):
                        dve.wait_ge(s_full, p * 4 + c + 1)
                        st.link(V.reduce_max(stm[:, c, 0:1], ps[:, c, :], AX))
                        V.tensor_scalar(stm[:, c, 1:2], stm[:, c, 0:1], -MLA_SCALE, None, ALU.mult).then_inc(s_max, 1)
                    for c in range(4):
                        dve.wait_ge(s_exp, p * 4 + c + 1)
                        st.link(V.reciprocal(stm[:, c, 3:4], stm[:, c, 2:3]))
                        V.tensor_scalar(Pm[:, c, :], Pm[:, c, :], stm[:, c, 3:4], None, ALU.mult).then_inc(p_ready, 1)
                    dve.wait_ge(pv_full, p + 1)
                    zs = view(ozm, (1, T), at=p * T)
                    V.tensor_tensor(zs, ps[:, 6, :], zs, ALU.mult).then_inc(pv_kept, 1)

        def in_vector(dve, st, l):
            b = base(l)
            wait_strip(dve, f"in{l}", 0, 0)
            V.tensor_copy(vb.rearrange("p g c -> p (g c)"), ps[:, 1, :]).then_inc(in_dve_kept, 1)
            for s, buf, bank in ((3, ub, 6), (4, fb, 0)):
                for n in range(2 - l):
                    if n == 0 and l == 0:
                        dve.wait_ge(in_full, b["full"] + 1 + s)
                    else:
                        wait_strip(dve, f"in{l}", s, 0)
                    g = 2 * l + 2 * n
                    V.tensor_copy(buf[:, g:g + 2, :], ps[:, bank + n, :]).then_inc(in_dve_kept, 1)
            dve.wait_ge(rot_full, b["rot"] + 1)
            rope_vector(st, kb[:, CTX:T], kb[:, CTX:T], ps[:, 2, 0:LAT], cosb, sinb, k_rot).then_inc(qj_ready, 1)

        def attend_vector(dve, st, l):
            b = base(l)
            groups = range(2 * l, NG)
            nc_ = 2 * len(groups)
            combos = [(h2, g) for h2 in range(2) for g in groups]
            lat0 = CTX * (1 - l)
            with st.loop(0, 4, 1 + 4 * nc_) as j:
                dve.wait_ge(rot_full, j + (b["rot"] + 2))
                raw = view(q_raw, (1, LAT), at=j * T + lat0)
                V.tensor_tensor(q_rot, ps[:, 0, 0:LAT], sinb, ALU.mult)
                if l == 0:
                    V.tensor_copy(qj[:, 0:CTX], view(q_raw, (1, CTX), at=j * T))
                st.link(V.tensor_tensor(qj[:, CTX:T], raw, cosb, ALU.mult))
                V.tensor_tensor(qj[:, CTX:T], qj[:, CTX:T], q_rot, ALU.add).then_inc(qj_ready, 1)

                def top(c):
                    h2, g = combos[c]
                    nk = CTX if g < 2 else T
                    x = sc[:, c % 4, 0:nk]
                    dve.wait_ge(s_full, j * nc_ + (b["combo"] + c + 1))
                    if c >= 4:
                        dve.wait_ge(pt_full, j * nc_ + (b["combo"] + c - 3))
                    if g < 2:
                        st.link(V.tensor_scalar(x, ps[:, 2 + c % 4, 0:nk], ATT_SCALE, None, ALU.mult))
                    else:
                        st.link(V.scalar_tensor_tensor(x, ps[:, 2 + c % 4, 0:nk], ATT_SCALE, amask[:, g - 2, :], ALU.mult, ALU.add))
                    st.link(V.reduce_max(stb[:, c % 4, 0:1], x, AX))
                    V.tensor_scalar(stb[:, c % 4, 1:2], stb[:, c % 4, 0:1], sink[:, bass.ds(j + (l * 8 + h2 * 4), 1)], -1.0,
                                    ALU.max, ALU.mult).then_inc(s_max, 1)

                def norm(c):
                    h2, g = combos[c]
                    nk = CTX if g < 2 else T
                    dve.wait_ge(s_exp, j * nc_ + (b["combo"] + c + 1))
                    st.link(V.tensor_tensor(stb[:, c % 4, 4:5], stb[:, c % 4, 2:3], stb[:, c % 4, 3:4], ALU.add))
                    st.link(V.reciprocal(stb[:, c % 4, 5:6], stb[:, c % 4, 4:5]))
                    V.tensor_scalar(sc[:, c % 4, 0:nk], sc[:, c % 4, 0:nk], stb[:, c % 4, 5:6], None, ALU.mult).then_inc(p_ready, 1)

                top(0)
                top(1)
                for s in range(nc_ // 2):
                    if 2 * s + 2 < nc_:
                        top(2 * s + 2)
                        top(2 * s + 3)
                    norm(2 * s)
                    norm(2 * s + 1)
                if l == 0:
                    dve.wait_ge(mod_turned, j * 12 + (mod_turn["mod1"] * 12 + 12))
                    V.tensor_tensor(view(mod_b[1], (2, 12), (1, 2), at=j * 24), ps[:, 0, 0:24].rearrange("p (m c) -> p m c", c=2),
                                    view(vecs, (1, 12), (0, 2), at=j * 12 + MODB + 48), ALU.add).then_inc(mod_ready, 1)

        def branches_vector(dve, l):
            b = base(l)
            ns = 2 - l
            for gp in range(2):
                dve.wait_ge(br_full, b["br"] + gp + 1)
                V.tensor_copy(pooled[:, gp, l * 256:T], ps[:, gp, l * 256:T]).then_inc(br_dve_kept, 1)
            for n in range(2 * ns):
                dve.wait_ge(br_full, b["br"] + 3 + n)
                if n >= 2:
                    dve.wait_ge(br_full, b["br"] + 4 + 2 * ns + n - 1)
                V.tensor_copy(fcs[:, n % 2, :], ps[:, 2 + n, :]).then_inc(br_dve_kept, 1)

        def merge_vector(dve, st, l):
            n, c0 = T - CTX * l, CTX * l
            with st.loop(0, 4, 2) as t:
                for m in range(2):
                    M = t * 2 + m
                    dve.wait_ge(y_ready, raised(M + 8 * l))
                    for j in range(3):
                        dve.wait_ge(gates_ready, raised(M * 3 + (24 * l + j + 1)))
                        wait_merge(dve, l, t, m, 3 + j)
                        ins = V.tensor_tensor(brg[:, j, 0:n], ps[:, 3 + j, 0:n], gts[:, j, 0:n], ALU.mult)
                    ins.then_inc(mg_read, 1)
                    dve.wait_ge(mg_read, raised(M + (8 * l + 1)))
                    st.link(V.tensor_tensor(brg[:, 0, 0:n], brg[:, 0, 0:n], brg[:, 1, 0:n], ALU.add))
                    V.tensor_tensor(view(yT, (1, n), at=M * T + c0), brg[:, 0, 0:n], brg[:, 2, 0:n], ALU.add).then_inc(y_ready, 1)

        def add_gated(k, bank, gate, l):
            for c in range(l, 2):
                cols = view(xT, (1, 256), at=k * T + c * 256)
                ins = V.scalar_tensor_tensor(cols, ps[:, bank, (c - l) * 256:(c - l) * 256 + 256],
                                             gate(k, c), cols, ALU.mult, ALU.add)
            ins.then_inc(x_added, 1)

        def out_vector(dve, l):
            for j in range(4):
                for m in range(2):
                    k = 2 * j + m
                    if m == 0:
                        dve.wait_ge(out_full, 4 * l + j + 1)
                    else:
                        wait_strip(dve, f"out{l}", j, 0)
                    add_gated(k, k, lambda k, c: mod_b[l][:, 16 + k, c:c + 1], l)

        def up_vector(dve, st, l):
            n, ns = T - CTX * l, 2 - l
            def tap(k, f, part):
                return vecs[:, bass.ds(f + (CONV + (l * 3 + k) * 44 + part * FT), 1)]
            with st.loop(0, FT // 2, 4) as t:
                for j in range(2):
                    f = t * 2 + j
                    dve.wait_ge(tap_ready, f * 2 + (2 * FT * l + 2))
                    for k, (d0, s0) in ((0, (1, 0)), (2, (0, 1))):
                        for part in range(2):
                            a = 2 * j + part
                            dst = view(acc, (256, ns), (1, 255), at=a * T + d0)
                            src = ps[:, a, 0:n].rearrange("p (s t) -> p s t", s=ns)[:, :, s0:s0 + 255]
                            ins = V.scalar_tensor_tensor(dst, src, tap(k, f, part), dst, ALU.mult, ALU.add)
                        if k == 0:
                            st.link(ins)
                        else:
                            ins.then_inc(conv_ready, 1)
                for j in range(2):
                    f = t * 2 + j
                    dve.wait_ge(sf_ready, f + (FT * l + 1))
                    st.link(V.tensor_tensor(acc[:, 2 * j, 0:n], acc[:, 2 * j, 0:n], acc[:, 2 * j + 1, 0:n], ALU.mult))
                    V.tensor_tensor(view(hid, (1, n), at=f * T), acc[:, 2 * j, 0:n], sgf[:, j, 0:n], ALU.mult).then_inc(hid_ready, 1)

        def down_vector(dve, l):
            with dve.Fori(0, 2) as t:
                for j in range(4):
                    wait_strip(dve, f"down{l}", j, t)
                    add_gated(t * 4 + j, j, lambda k, c: view(mod_b[l], (1, 1), at=(k + 40) * 2 + c), l)

        @block.vector
        def _(dve):
            st = Steps(dve, dve_step)
            V.memset(ones[1024], 1.0 / 1024)
            V.memset(ones[256], 1.0 / 256)
            V.memset(ones[128], 1.0 / 128)
            V.memset(eps, EPS)
            for n, raised_sem in enumerate((rt_ready, o_ready, z_kept, pt_kept, pv_kept, gates_ready, mg_read, y_ready, hid_ready, o_full)):
                V.memset(raise_at[:, n:n + 1], 0.0).then_inc(raised_sem, 1)
            for k in range(KT):
                dve.wait_ge(x_turned, k + 1)
                V.tensor_copy(xT[:, k, :], ps[:, k % 4, :]).then_inc(x_copied, 1)
            dve.wait_ge(msk_loaded, 16)
            dve.wait_ge(vec_loaded, 16 * N_VEC)
            dve.wait_ge(vec_turned, 1)
            V.tensor_copy(vecs[:, 0:432], ps[:, 6, 0:432])
            V.tensor_copy(vecs[:, 432:520], ps[:, 7, 0:88]).then_inc(vec_ready, 1)
            dve.wait_ge(sig_c, 1)
            V.tensor_tensor(sil, sil, vecs[:, 0:32], ALU.mult).then_inc(sil_ready, 1)
            xcol = lambda k: xT[:, k, :]
            norm_vector(dve, st, "hg_pre", T)
            normed_vector("hg_pre", xcol, 0, T)
            mod_vector(dve, "ada0", 2, mod_a[0], ADAB)
            dve.wait_ge(mod_ready, 1)
            modulate_coef(st, mod_a[0][:, 8:16, :], vecs[:, PRE:PRE + 8])
            for idx in range(4, 8):
                hg_gate_vector(dve, 0, idx)
            hg_unpack_vector(dve, st, 0)

            def core(i, gates):
                hg_scores_vector(dve, st, i, 0)
                for term in range(1, 8):
                    hg_scores_vector(dve, st, i, term)
                    if gates and term >= 4:
                        hg_gate_vector(dve, i + 1, term)
                hg_states_vector(dve, st, i)
                if gates:
                    hg_unpack_vector(dve, st, i + 1)
                hg_read_vector(dve, st, i)
            with st.loop(1, PAIRS, LEVELS + 4) as i:
                core(i - 1, True)
            core(PAIRS - 1, False)
            dve.wait_ge(h_ready, h_end["hg_pre"])
            post_vector(dve, st, "hg_post", mod_a[0][:, 16:24, :], vecs[:, POST:POST + 8], 0, T)
            norm_vector(dve, st, "mla_pre", T)
            normed_vector("mla_pre", xcol, 0, T)
            mod_vector(dve, "ada1", 2, mod_a[1], ADAB + 24)
            dve.wait_ge(mod_ready, 2)
            dve.wait_ge(x_added, 8)
            modulate_coef(st, mod_a[1][:, 8:16, :], vecs[:, PRE + 8:PRE + 16])
            mla_vector(dve, st)
            for n in range(4):
                dve.wait_ge(x_turned, KT + n + 1)
                V.tensor_copy(xT[:, 2 * n:2 * n + 2, 0:CTX], ps[:, 4 + n, :].rearrange("p (k t) -> p k t", k=2)).then_inc(x_copied, 1)
            dve.wait_ge(h_ready, h_end["mla_pre"])
            post_vector(dve, st, "mla_post", mod_a[1][:, 16:24, :], vecs[:, POST + 8:POST + 16], CTX, LAT)
            for l in range(2):
                n, c0 = T - CTX * l, CTX * l
                def mix_coef():
                    dve.wait_ge(x_added, 16 + 16 * l)
                    modulate_coef(st, mod_b[l][:, 8:16, :], vecs[:, MIX + 8 * l:MIX + 8 * l + 8])

                if l == 1:
                    dve.wait_ge(mod_ready, 7)
                    mix_coef()
                norm_vector(dve, st, f"mix{l}", T)
                normed_vector(f"mix{l}", xcol, 0, T)
                if l == 0:
                    mod_vector(dve, "mod0", 4, mod_b[0], MODB)
                    dve.wait_ge(mod_ready, 3)
                    mix_coef()
                in_vector(dve, st, l)
                attend_vector(dve, st, l)
                branches_vector(dve, l)
                merge_vector(dve, st, l)
                out_vector(dve, l)
                dve.wait_ge(h_ready, h_end[f"mix{l}"])
                modulate_coef(st, mod_b[l][:, 32:40, :], vecs[:, FFN + 8 * l:FFN + 8 * l + 8])
                norm_vector(dve, st, f"ffn{l}", n)
                normed_vector(f"ffn{l}", lambda k: xT[:, k, c0:T], c0, T)
                up_vector(dve, st, l)
                down_vector(dve, l)
            norm_vector(dve, st, "final", LAT)
            normed_vector("final", lambda k: xT[:, k, CTX:T], 0, LAT)
            for n in range(4):
                dve.wait_ge(o_turned, n + 1)
                V.tensor_copy(o_out[:, :, n * 256:n * 256 + 256].rearrange("p g (k f) -> p k g f", k=2),
                              ps[:, n, :].rearrange("p (k g f) -> p k g f", k=2, g=2)).then_inc(out_kept, 1)

        def move_pool(pool, i):
            if not (isinstance(i, int) and i == 0):
                pool.wait_ge(o_full, raised(i * 2))
                pool.wait_ge(st_ready, i)
            wait_apart(pool, act_freed, i * 6 + 6)
            nc.gpsimd.tensor_copy(Tw, f_st.rearrange("p d c -> p (d c)"))
            nc.gpsimd.tensor_copy(v_w, v_st).then_inc(moved, 1)

        @block.gpsimd
        def _(pool):
            pool.dma_start(ident, const["ident"]).then_inc(tab_loaded, 16)
            pool.dma_start(masks_i, const["masks"]).then_inc(msk_loaded, 16)
            move_pool(pool, 0)
            with pool.Fori(1, PAIRS) as i:
                move_pool(pool, i)
            pool.wait_ge(o_ready, raised(2 * PAIRS))
            pool.dma_start(ctx2_in, w["ctx_2"][0].rearrange("(g p) d -> p g d", p=128)).then_inc(ctx2_loaded, 16)
            nc.gpsimd.memset(poolw, 0.0).then_inc(pool_step, 1)
            for dst, name in ((cosb, "cosb"), (sinb, "sinb"), (rotb, "rotb"), (cosm, "cosm"), (sinm, "sinm"), (rotm, "rotm"),
                              (amask, "amask"), (poolm, "poolm"), (dftm, "dftm"), (dftc, "dftc")):
                pool.dma_start(dst, const[name]).then_inc(tab_loaded, 16)
            pool.wait_ge(pool_step, 1)
            for l in range(2):
                for g in range(4):
                    e = g % 2 * 64
                    pool.dma_start(poolw[e:e + 64, l, g // 2, e:e + 64], w["pool_w_2"][l, g]).then_inc(tab_loaded, 16)



def tables():
    f = np.float32
    out = {"ident": np.eye(128, dtype=f)}
    t = np.arange(128)
    masks = np.zeros((128, LEVELS, 128), np.int32)
    for l in range(LEVELS):
        masks[:, l, :] = ((t[:, None] >> (l + 1)) == (t[None, :] >> (l + 1))) & ((t[:, None] >> l) != (t[None, :] >> l))
    out["masks"] = masks
    pos = np.arange(LAT, dtype=np.float32)
    row, col = np.floor(pos / 64).astype(f), (pos % 64).astype(f)
    inv = (np.float32(10000.0) ** (-np.arange(0, 32, 2, dtype=f) / np.float32(32))).astype(f)
    ang = np.concatenate([row[:, None] * inv, col[:, None] * inv], axis=-1)
    out["cosm"] = np.tile(np.cos(ang).T, (4, 1)).astype(f)
    out["sinm"] = np.tile(np.sin(ang).T, (4, 1)).astype(f)

    def turn(half):
        r = np.zeros((128, 128), f)
        for p in range(128):
            if (p // half) % 2 == 0:
                r[p + half, p] = -1
            else:
                r[p - half, p] = 1
        return r

    out["rotm"] = turn(32)
    inv = (np.float32(10000.0) ** (-np.arange(16, dtype=f) / np.float32(16))).astype(f)
    ang = np.stack([row[:, None] * inv, col[:, None] * inv], axis=1)
    full = np.repeat(ang[:, :, None, :], 2, axis=2).reshape(LAT, 64)
    out["cosb"] = np.tile(np.cos(full).T, (2, 1)).astype(f)
    out["sinb"] = np.tile(np.sin(full).T, (2, 1)).astype(f)
    out["rotb"] = turn(16)
    am = np.zeros((128, 2, T), f)
    q = np.arange(LAT).reshape(2, 128)
    for g in range(2):
        am[:, g, CTX:] = np.where(np.abs(q[g][:, None] - np.arange(LAT)[None, :]) <= 128, 0, -1e30)
    out["amask"] = am
    pm = np.zeros((LAT, 4, LAT), np.float64)
    for g, win in enumerate((2, 4, 8, 16)):
        for u in range(LAT):
            lo, hi = max(u - win // 2, 0), min(u - win // 2 + win, LAT)
            pm[lo:hi, g, u] = 1.0 / (hi - lo)
            pm[u, g, u] -= 1.0
    out["poolm"] = pm.reshape(2, 128, 4, LAT).transpose(1, 0, 2, 3).astype(f)
    ang = 2 * np.pi * ((np.arange(256)[:, None] * np.arange(256)[None, :]) % 256) / 256
    dt = np.concatenate([np.cos(ang), np.sin(ang)], axis=1) / 16
    out["dftm"] = dt.reshape(2, 128, 512).transpose(1, 0, 2).astype(f)
    ang = 2 * np.pi * ((np.arange(64)[:, None] * np.arange(64)[None, :]) % 64) / 64
    dc = np.zeros((128, 2, 128))
    for e in (0, 64):
        dc[e:e + 64, 0, e:e + 64] = np.cos(ang) / 8
        dc[e:e + 64, 1, e:e + 64] = -np.sin(ang) / 8
    out["dftc"] = dc.astype(f)
    return {k: np.ascontiguousarray(v) for k, v in out.items()}


_INS = ["x", "c", "ctx", "c_ctx", "ctx_2", "ada_w", "ada_b", "norm_pre", "norm_post", "hg_w_in", "hg_o_norm", "hg_w_out",
        "mla_w_in", "mla_qa_norm", "mla_w_qb", "mla_kva_norm", "mla_w_kvb", "mla_w_out", "c_2", "c_ctx_2", "w_mod_2",
        "b_mod_2", "norm_mix_2", "norm_ffn_2", "w_in_2", "attn_sink_2", "pool_w_2", "pool_scale_2", "w_br_attn_2",
        "w_br_pool_2", "w_br_four_2", "w_out_2", "w_up_2", "conv_w_2", "w_down_2", "norm_final_2"]


def kernel(**inputs):
    import concourse.bacc as _bacc
    from concourse.bass_utils import run_bass_kernel_spmd as _run

    nc = _bacc.Bacc("TRN2", target_bir_lowering=False, num_devices=1)
    arrays = {}

    def give(name, a):
        a = np.ascontiguousarray(a)
        arrays[name] = a
        return nc.dram_tensor(name, a.shape, mybir.dt.from_np(a.dtype), kind="ExternalInput").ap()

    w = {name: give(f"in_{name}_dram", inputs[name]) for name in _INS}
    const = {name: give(f"table_{name}_dram", a) for name, a in tables().items()}
    out = nc.dram_tensor("out_dram", (1, LAT, D), mybir.dt.float32, kind="ExternalOutput").ap()
    build(nc, w, const, out)
    r = _run(nc, [arrays], core_ids=[0])
    return r.results[0]["out_dram"]
```
